# Optimizing a Trainium2 kernel written in Bass

```python
import jax, jax.numpy as jnp
from jax import lax
import numpy as np

D_MODEL = 1024
BATCH = 1
SEQ = 1024
DEPTH = 1

CHUNK = 64
GDN_HEADS = 4
GDN_DK = 128
GDN_DV = 128
GDN_CONV = 4
SWA_Q_HEADS = 8
SWA_KV_HEADS = 2
SWA_HEAD_DIM = 64
WINDOW = 128
WIN_CHUNKS = WINDOW // CHUNK
D_MIX = GDN_HEADS * GDN_DV + SWA_Q_HEADS * SWA_HEAD_DIM
GDN_QKV = 2 * GDN_HEADS * GDN_DK + GDN_HEADS * GDN_DV
GDN_Z = GDN_HEADS * GDN_DV
SWA_Q = SWA_Q_HEADS * SWA_HEAD_DIM
SWA_KV = SWA_KV_HEADS * SWA_HEAD_DIM
D_PROJ = GDN_QKV + GDN_Z + 2 * GDN_HEADS + SWA_Q + 2 * SWA_KV
N_GROUPS = 4
EXPERTS_PER_GROUP = 4
N_EXPERTS = N_GROUPS * EXPERTS_PER_GROUP
TOP_K = 2
D_EXPERT = 256
EPS = 1e-6

kernel_name = "hybrid_gdn_swa_sink_hier_moe"

def rms_norm(x, g):
    xf = x.astype(jnp.float32)
    y = xf * lax.rsqrt(jnp.mean(xf * xf, axis=-1, keepdims=True) + EPS)
    return (y * g.astype(jnp.float32)).astype(x.dtype)

def l2_norm(x):
    return x * lax.rsqrt(jnp.sum(x * x, axis=-1, keepdims=True) + EPS)

def causal_depthwise_conv(x, w):
    kw, cc = w.shape
    return lax.conv_general_dilated(
        x, w[:, None, :].astype(x.dtype), window_strides=(1,), padding=[(kw - 1, 0)],
        dimension_numbers=('NWC', 'WIO', 'NWC'), feature_group_count=cc)

def gated_delta_rule(q, k, v, log_a, beta):
    bb, t, h, kd = q.shape
    vd = v.shape[-1]
    c = CHUNK
    n = t // c
    q = (q * kd ** -0.5).reshape(bb, n, c, h, kd)
    k = k.reshape(bb, n, c, h, kd)
    v = v.reshape(bb, n, c, h, vd)
    beta = beta.reshape(bb, n, c, h)
    g = jnp.cumsum(log_a.reshape(bb, n, c, h), axis=2)
    g_last = g[:, :, -1]
    idx = jnp.arange(c)
    causal = idx[:, None] >= idx[None, :]
    strict = idx[:, None] > idx[None, :]
    gt = jnp.swapaxes(g, 2, 3)
    decay = jnp.exp(jnp.where(causal, gt[..., :, None] - gt[..., None, :], -jnp.inf))
    kb = k * beta[..., None]
    a_kk = jnp.where(strict, jnp.einsum('bnihd,bnjhd->bnhij', kb, k) * decay, 0.0)
    eye = jnp.eye(c, dtype=q.dtype)
    lower = eye + a_kk
    t_inv = lax.linalg.triangular_solve(lower, jnp.broadcast_to(eye, lower.shape),
                                        left_side=True, lower=True, unit_diagonal=True)
    u = jnp.einsum('bnhij,bnjhv->bnhiv', t_inv, v * beta[..., None])
    w = jnp.einsum('bnhij,bnjhd->bnhid', t_inv, kb * jnp.exp(g)[..., None])
    qk = jnp.einsum('bnihd,bnjhd->bnhij', q, k) * decay
    q_dec = jnp.einsum('bnihd->bnhid', q * jnp.exp(g)[..., None])
    k_dec = jnp.einsum('bnihd->bnhid', k * jnp.exp(g_last[:, :, None] - g)[..., None])
    chunk_dec = jnp.exp(g_last)

    def step(s, xs):
        u_n, w_n, q_n, qk_n, k_n, d_n = xs
        v_new = u_n - jnp.einsum('bhid,bhdv->bhiv', w_n, s)
        o_n = jnp.einsum('bhid,bhdv->bhiv', q_n, s) + jnp.einsum('bhij,bhjv->bhiv', qk_n, v_new)
        s = s * d_n[..., None, None] + jnp.einsum('bhid,bhiv->bhdv', k_n, v_new)
        return s, o_n

    xs = tuple(jnp.moveaxis(a, 1, 0) for a in (u, w, q_dec, qk, k_dec, chunk_dec))
    s0 = jnp.zeros((bb, h, kd, vd), q.dtype)
    _, o = lax.scan(step, s0, xs)
    return jnp.einsum('nbhcv->bnchv', o).reshape(bb, t, h, vd)

def swa_sink_attention(q, k, v, sinks):
    bb, t, hq, dh = q.shape
    hkv = k.shape[2]
    grp = hq // hkv
    c = CHUNK
    n = t // c
    qc = q.reshape(bb, n, c, hkv, grp, dh)
    kc = k.reshape(bb, n, c, hkv, dh)
    vc = v.reshape(bb, n, c, hkv, dh)

    def band(a):
        return jnp.concatenate(
            [jnp.pad(a, ((0, 0), (o, 0), (0, 0), (0, 0), (0, 0)))[:, :n]
             for o in range(WIN_CHUNKS - 1, -1, -1)], axis=2)

    kb, vb = band(kc), band(vc)
    s = jnp.einsum('bnqhgd,bnkhd->bnhgqk', qc, kb).astype(jnp.float32) * dh ** -0.5
    key_chunk = jnp.arange(n)[:, None] - (WIN_CHUNKS - 1 - jnp.arange(WIN_CHUNKS * c) // c)[None, :]
    valid = key_chunk >= 0
    s = jnp.where(valid[None, :, None, None, None, :], s, -jnp.inf)
    sk = sinks.astype(jnp.float32).reshape(hkv, grp)[None, None, :, :, None]
    m = jnp.maximum(s.max(-1), sk)
    p = jnp.exp(s - m[..., None])
    denom = p.sum(-1) + jnp.exp(sk - m)
    o = jnp.einsum('bnhgqk,bnkhd->bnqhgd', (p / denom[..., None]).astype(v.dtype), vb)
    return o.reshape(bb, t, hq * dh)

def hier_moe(h, w_group, b_group, w_expert, b_expert, w_gate_up, w_down):
    bb, t, d = h.shape
    tok = h.reshape(-1, d)
    gl = (tok @ w_group).astype(jnp.float32) + b_group.astype(jnp.float32)
    p_group = jax.nn.softmax(gl, axis=-1)
    p_top, g_idx = lax.top_k(p_group, 1)
    el = ((tok @ w_expert).astype(jnp.float32) + b_expert.astype(jnp.float32)
          ).reshape(-1, N_GROUPS, EXPERTS_PER_GROUP)
    el_sel = jnp.take_along_axis(el, g_idx[:, :, None], axis=1)[:, 0]
    e_val, e_idx = lax.top_k(el_sel, TOP_K)
    e_w = jax.nn.softmax(e_val, axis=-1) * p_top
    flat_idx = g_idx * EXPERTS_PER_GROUP + e_idx
    gates = jnp.einsum('nk,nke->ne', e_w, jax.nn.one_hot(flat_idx, N_EXPERTS, dtype=jnp.float32))
    y = jnp.zeros_like(tok)
    for e in range(N_EXPERTS):
        gu = tok @ w_gate_up[e]
        act = jax.nn.silu(gu[:, :D_EXPERT]) * gu[:, D_EXPERT:]
        y = y + gates[:, e:e + 1].astype(tok.dtype) * (act @ w_down[e])
    return y.reshape(bb, t, d)

def setup_inputs(seed: int = 0) -> dict:
    key = jax.random.key(seed)
    ks = jax.random.split(key, 20)
    f32 = jnp.float32
    nrm = lambda k, shape, s: jax.random.normal(k, shape, f32) * s
    dt = jnp.exp(jax.random.uniform(ks[4], (DEPTH, GDN_HEADS), f32, np.log(1e-3), np.log(1e-1)))
    return {
        "x": jax.random.normal(ks[0], (BATCH, SEQ, D_MODEL), f32),
        "attn_norm_g": 1.0 + nrm(ks[1], (DEPTH, D_MODEL), 0.02),
        "w_in": nrm(ks[2], (DEPTH, D_MODEL, D_PROJ), D_MODEL ** -0.5),
        "conv_w": nrm(ks[3], (DEPTH, GDN_CONV, GDN_QKV), GDN_CONV ** -0.5),
        "gdn_a_log": jnp.log(jax.random.uniform(ks[5], (DEPTH, GDN_HEADS), f32, 1.0, 16.0)),
        "gdn_dt_bias": dt + jnp.log(-jnp.expm1(-dt)),
        "gdn_out_norm_g": 1.0 + nrm(ks[6], (DEPTH, GDN_DV), 0.02),
        "swa_q_norm_g": 1.0 + nrm(ks[7], (DEPTH, SWA_HEAD_DIM), 0.02),
        "swa_k_norm_g": 1.0 + nrm(ks[8], (DEPTH, SWA_HEAD_DIM), 0.02),
        "swa_sinks": nrm(ks[9], (DEPTH, SWA_Q_HEADS), 0.5),
        "w_out": nrm(ks[10], (DEPTH, D_MIX, D_MODEL), D_MIX ** -0.5),
        "ffn_norm_g": 1.0 + nrm(ks[11], (DEPTH, D_MODEL), 0.02),
        "w_group": nrm(ks[12], (DEPTH, D_MODEL, N_GROUPS), D_MODEL ** -0.5),
        "b_group": nrm(ks[13], (DEPTH, N_GROUPS), 0.01),
        "w_expert": nrm(ks[14], (DEPTH, D_MODEL, N_EXPERTS), D_MODEL ** -0.5),
        "b_expert": nrm(ks[15], (DEPTH, N_EXPERTS), 0.01),
        "w_gate_up": nrm(ks[16], (DEPTH, N_EXPERTS, D_MODEL, 2 * D_EXPERT), D_MODEL ** -0.5),
        "w_down": nrm(ks[17], (DEPTH, N_EXPERTS, D_EXPERT, D_MODEL), D_EXPERT ** -0.5),
    }

def reference(x, attn_norm_g, w_in, conv_w, gdn_a_log, gdn_dt_bias, gdn_out_norm_g,
              swa_q_norm_g, swa_k_norm_g, swa_sinks, w_out, ffn_norm_g, w_group, b_group,
              w_expert, b_expert, w_gate_up, w_down):
    f32 = jnp.float32
    bb, t, _ = x.shape
    s1 = GDN_QKV
    s2 = s1 + GDN_Z
    s3 = s2 + GDN_HEADS
    s4 = s3 + GDN_HEADS
    s5 = s4 + SWA_Q
    s6 = s5 + SWA_KV
    for l in range(DEPTH):
        h = rms_norm(x, attn_norm_g[l])
        proj = h @ w_in[l]
        a_qkv, a_z, a_alpha, a_beta, b_q, b_k, b_v = jnp.split(proj, [s1, s2, s3, s4, s5, s6], axis=-1)

        qkv = jax.nn.silu(causal_depthwise_conv(a_qkv, conv_w[l])).astype(f32)
        fq, fk, fv = jnp.split(qkv, [GDN_HEADS * GDN_DK, 2 * GDN_HEADS * GDN_DK], axis=-1)
        gq = l2_norm(fq.reshape(bb, t, GDN_HEADS, GDN_DK))
        gk = l2_norm(fk.reshape(bb, t, GDN_HEADS, GDN_DK))
        gv = fv.reshape(bb, t, GDN_HEADS, GDN_DV)
        log_a = -jnp.exp(gdn_a_log[l].astype(f32)) * jax.nn.softplus(
            a_alpha.astype(f32) + gdn_dt_bias[l].astype(f32))
        beta = jax.nn.sigmoid(a_beta.astype(f32))
        o_a = gated_delta_rule(gq, gk, gv, log_a, beta)
        o_a = rms_norm(o_a, gdn_out_norm_g[l]) * jax.nn.silu(
            a_z.astype(f32).reshape(bb, t, GDN_HEADS, GDN_DV))
        y_a = o_a.reshape(bb, t, GDN_HEADS * GDN_DV).astype(x.dtype)

        sq = rms_norm(b_q.reshape(bb, t, SWA_Q_HEADS, SWA_HEAD_DIM), swa_q_norm_g[l])
        sk = rms_norm(b_k.reshape(bb, t, SWA_KV_HEADS, SWA_HEAD_DIM), swa_k_norm_g[l])
        sv = b_v.reshape(bb, t, SWA_KV_HEADS, SWA_HEAD_DIM)
        y_b = swa_sink_attention(sq, sk, sv, swa_sinks[l]).astype(x.dtype)

        x = x + jnp.concatenate([y_a, y_b], axis=-1) @ w_out[l]

        x = x + hier_moe(rms_norm(x, ffn_norm_g[l]), w_group[l], b_group[l], w_expert[l],
                         b_expert[l], w_gate_up[l], w_down[l])
    return x


_drawn_inputs = setup_inputs


def setup_inputs(seed=0):
    import zlib

    import numpy as np

    out = dict(_drawn_inputs(seed))
    spreads = {}
    factors = {'attn_norm_g': 2.721,
     'gdn_out_norm_g': 13.13,
     'swa_q_norm_g': 8.0,
     'swa_k_norm_g': 8.0,
     'swa_sinks': 8.0,
     'b_group': 64.0,
     'b_expert': 64.0,
     'ffn_norm_g': 8.0}
    for name, (base, spread) in spreads.items():
        noise = np.random.default_rng([zlib.crc32(name.encode()), seed]).standard_normal(out[name].shape)
        drawn = base * np.exp(spread * noise) if base else spread * noise
        out[name] = __import__('jax').numpy.asarray(drawn.astype(out[name].dtype))
    for name, factor in factors.items():
        out[name] = (out[name] * factor).astype(out[name].dtype)
    return out
```

```python
from collections import namedtuple
from contextlib import ExitStack

import numpy as np

import concourse.bass as bass
from concourse import mybir

F32 = mybir.dt.float32
I32 = mybir.dt.int32
ALU = mybir.AluOpType
ACT = mybir.ActivationFunctionType
AX_X = mybir.AxisListType.X
P = 128
EPS = 1e-6

D = 1024
T = 1024
NT = T // P
KD = D // P
H = 4
HP = H * P
DPROJ = 2824
QH, KVH, DH = 8, 2, 64
GRP = QH // KVH
CH = 64
QK = (QH + KVH) * DH
Z0, AL0, BE0, SQ0 = 0, HP, HP + H, HP + 2 * H
SK0 = SQ0 + QH * DH
SV0 = SK0 + KVH * DH
TAIL = SV0 + KVH * DH
CHUNKS = [(0, 512), (512, 512), (1024, 512), (1536, 512), (2048, 512), (2560, 264)]
NC_ = len(CHUNKS)
KW = 4
HALO = KW - 1
GROUPS, EPG, NE, DE = 4, 4, 16, 256
NL = GROUPS + NE
TOPK = 2
SLOT_TILES = (TOPK * T - NE) // P + NE
LEVELS = [2, 4, 8, 16, 32, 64]
RSQRT_MAGIC = 0x5F3759DF
NSMALL = 16
VF, VB = 35, 49
BIG = 1e30


def build(nc, x, attn_norm_g, w_in, conv_w, a_log, dt_bias, out_norm_g, q_norm_g, k_norm_g, sinks,
          w_out, ffn_norm_g, w_group, b_group, w_expert, b_expert, w_gate_up, w_down, out, dbg=None):
    with ExitStack() as ctx:
        def sb(name, shape, dt=F32):
            return ctx.enter_context(nc.sbuf_tensor(name, [P] + shape, dt))

        def sems(names, about=""):
            return namedtuple("Signals", names)(*[ctx.enter_context(nc.semaphore(about + n)) for n in names.split()])

        x_mid = nc.dram_tensor("x_mid", [T, D], F32).ap()
        h_mid = nc.dram_tensor("h_mid", [T, D], F32).ap()
        y_slots = nc.dram_tensor("y_slots", [SLOT_TILES * P, D], F32).ap()

        w_sb = sb("w_sb", [KD, DPROJ])
        wo_sb = sb("wo_sb", [KD, D])
        ident = sb("ident", [P])
        ones = sb("ones", [P])
        upper = sb("upper", [P])
        upper_strict = sb("upper_strict", [P])
        level_mask = sb("level_mask", [1 + len(LEVELS), P])
        gain1 = sb("gain1", [KD])
        gain2 = sb("gain2", [KD])
        cw = sb("cw", [KW, 3 * H])
        rows = sb("rows", [2 * DH + P + 3 * H + QH + NL])
        GQ, GO, DT, AL, SI, BL = np.cumsum([0, 2 * DH, P, H, H, QH]).tolist()
        gqk = rows[:, GQ:GQ + 2 * DH]
        g_out = rows[:, GO:GO + P]
        dtb = rows[:, DT:DT + H]
        neg_a = rows[:, AL:AL + H]
        sink = rows[:, SI:SI + QH]
        b_rt = rows[:, BL:BL + NL]
        w_rt = sb("w_rt", [KD, NL])
        key_mask = sb("key_mask", [P])

        xt = sb("xt", [D])
        hT = sb("hT", [KD, P])
        pqkv = sb("pqkv", [3 * HP])
        tail = sb("tail", [TAIL])
        ci = sb("ci", [3 * H, HALO + P])
        cv = pqkv[:, :].rearrange("p (h n) -> p h n", n=P)
        qkvT = sb("qkvT", [3 * H, P])
        qkn = sb("qkn", [QH + KVH, DH])
        gsz = sb("gsz", [H, P])
        fs = sb("fs", [80])
        kn = sb("kn", [H, P])
        vt = sb("vt", [H, P])
        knT = sb("knT", [H, P])
        ctmp = sb("ctmp", [3 * H, P])
        dT, aT, XT = ctmp[:, 0:H, :], ctmp[:, H:2 * H, :], ctmp[:, 2 * H:3 * H, :]
        qkT = sb("qkT", [H, P])
        aTm = sb("aTm", [2, H, P])
        qkg = aTm[:, :, :, :].rearrange("p a h n -> p (a h n)")[:, 0:QK].rearrange("p (h n) -> p h n", n=DH)
        X = sb("X", [H, P])
        Y = sb("Y", [H, P])
        V = sb("V", [H, P])
        S = sb("S", [H, P])
        bs = sb("bs", [112])
        qT = V
        kWin = sb("kWin", [3, CH])
        vWin = sb("vWin", [2, KVH, DH + 1])
        lg = sb("lg", [NT, NL])
        free = w_sb[:, :, :].rearrange("p k n -> p (k n)")
        taken = [0]

        def part(*shape):
            n = int(np.prod(shape))
            a = free[:, taken[0]:taken[0] + n]
            taken[0] += n
            assert taken[0] <= KD * DPROJ
            if len(shape) == 2:
                return a.rearrange("p (a b) -> p a b", a=shape[0])
            if len(shape) == 3:
                return a.rearrange("p (a b c) -> p a b c", a=shape[0], b=shape[1])
            return a

        wgu = [part(KD, 2 * DE) for _ in range(2)]
        wdn = [part(DE // P, D) for _ in range(2)]
        hg = [part(D) for _ in range(2)]
        hgT = [part(KD, P) for _ in range(2)]
        yo = [part(D) for _ in range(2)]
        tnh, glu, gluT = part(DE), part(DE), part(DE // P, P)
        gmax, m1, m2, sump, gate1, gate2, seen = [part(NT) for _ in range(7)]
        og, es, e1, e2 = [part(NT, GROUPS) for _ in range(4)]
        ex = part(NT * GROUPS + NT)
        prod, pick1, pick2, both_picks = [part(NT, GROUPS, EPG) for _ in range(4)]
        run, slot = part(NT + 1, NE), part(NT, NE)
        over = part(NE, NT)
        tiles_of, tiles_to, base = part(NE), part(NE), part(NE)
        slots = part(TOPK * NT)
        slots_i, mod_i, div_i = [part(TOPK * NT).bitcast(I32) for _ in range(3)]
        mod_f, div_f = part(TOPK * NT), part(TOPK * NT)
        iota_i = part(P).bitcast(I32)
        iota_f, tok_f = part(P), part(NT)
        step_f = part(NT)
        past = part(SLOT_TILES + 1, NE)
        texp_f, texp = part(SLOT_TILES + 1), part(SLOT_TILES + 1).bitcast(I32)
        idx = part(SLOT_TILES + 1).bitcast(I32)
        hot_mod = [hgT[u // 8].rearrange("p k n -> p (k n)")[:, (u % 8) * P:(u % 8 + 1) * P] for u in range(TOPK * NT)]
        hot_div = yo[0][:, 0:TOPK * NT * 32].rearrange("p (u m) -> p u m", m=32)
        out_a = [wgu[b][:, 0:2, :].rearrange("p k n -> p (k n)") for b in range(2)]
        out_b = [wgu[b][:, 2:4, :].rearrange("p k n -> p (k n)") for b in range(2)]
        out_x = [wgu[b][:, 4:6, :].rearrange("p k n -> p (k n)") for b in range(2)]
        y_mix = sb("y_mix", [D])
        sc = sb("sc", [QH, P])
        pT = sb("pT", [QH, P])
        xr = sc[:, :, :].rearrange("p h n -> p (h n)")
        yT, hT2, r, o, o2, kd = pT, pT, vt, X, Y, kn

        pm = [ctx.enter_context(nc.psum_tensor(f"pm{i}", [P, 512], F32)) for i in range(8)]

        def heads(bank, n=P):
            return bank[:, 0:4 * n].rearrange("p (h n) -> p h n", h=4)

        def wide(ap4, n=P):
            return ap4.unsqueeze(2).broadcast_to([P, ap4.shape[1], n])

        L = sems("consts_loaded masks_made weights_ready state_zeroed dve_consts x_loaded xr_loaded mid_stored masked")
        w_loaded = [ctx.enter_context(nc.semaphore(f"w_loaded{c}")) for c in range(NC_)]
        wo_loaded = ctx.enter_context(nc.semaphore("wo_loaded"))
        F = sems("ssx_ready h_scaled h_turned hT_ready chunk_done chunk_copied turned ci_copied halo_ready"
                 " conv_done tanh_ready qkvT_ready sq_ready swa_squared swa_gained qkn_ready u_ready"
                 " exp_ready ln_ready la_ready tz_ready hz_ready gsz_ready front_step")
        B = sems("kv_turned small_done gi_done kn_ready vt_ready kn_turned knT_ready diff_ready dT_exp dT_ready"
                 " eg_ready kk_done qk_done aT_ready qkT_ready aTm_ready xT0_ready x0_turned x0_copied y_done"
                 " y_copied z_done x_updated ks_done r_ready v0_done v_ready o2_done kd_ready s_done s_updated"
                 " o_ready o_squared ya_ready swa_turned qT_ready kWin_ready kOld_ready vOld_ready vWin_ready scores_done"
                 " top_found sc_ready p_ready p_turned pT_ready pv_done sink_in sink_exp yb_ready y_turned yT_ready out_done"
                 " xm_ready ss2_ready hm_ready hm_turned hT2_ready logits_done lg_ready back_step h_free")

        R = sems("iotas route_step exp_in exp_out picks counts hots idx_summed idx_ready ready", "route_")
        M = sems("turned hT_ready gu_done tanh_ready glu_step glu_ready glu_turned gluT_ready down_done"
                 " y0_ready y1_ready half_summed summed", "slots_")
        gathered, w1_loaded, w2_loaded, y_stored, a_loaded, b_loaded, m_loaded, out_stored = [
            [ctx.enter_context(nc.semaphore(f"{n}{b}")) for b in range(2)]
            for n in "gathered w1_loaded w2_loaded y_stored a_loaded b_loaded m_loaded out_stored".split()]

        def run_slots(eng, step, last):
            step(0, 0, 0)
            with eng.Fori(0, SLOT_TILES // 2 - 1) as u:
                step(2 * u + 1, 1, u)
                step(2 * u + 2, 0, u + 1)
            step(SLOT_TILES - 2, 1, SLOT_TILES // 2 - 1)
            step(SLOT_TILES - 1, 0, SLOT_TILES // 2)
            last()

        block = ctx.enter_context(nc.Block())

        def later(t):
            return not isinstance(t, int) or t > 0

        def run_tiles(eng, front, both, back):
            front(0)
            both(0)
            with eng.Fori(1, NT - 1) as i:
                both(i)
            back(NT - 1)

        @block.sync
        def _(sp):
            def col(ap1, n):
                return ap1.rearrange("(k p) -> p k", p=P)

            small = [
                (gain1[:, :], attn_norm_g[0].rearrange("(k p) -> p k", p=P)),
                (gain2[:, :], ffn_norm_g[0].rearrange("(k p) -> p k", p=P)),
            ]
            small += [(cw[:, j, :], conv_w[0, j].rearrange("(k p) -> p k", p=P)) for j in range(KW)]
            small += [
                (gqk[:, 0:DH], q_norm_g.broadcast_to([P, DH])),
                (gqk[:, DH:2 * DH], k_norm_g.broadcast_to([P, DH])),
                (g_out, out_norm_g.broadcast_to([P, P])),
                (dtb, dt_bias.broadcast_to([P, H])),
                (neg_a, a_log.broadcast_to([P, H])),
                (sink, sinks.broadcast_to([P, QH])),
                (b_rt[:, 0:GROUPS], b_group.broadcast_to([P, GROUPS])),
                (b_rt[:, GROUPS:NL], b_expert.broadcast_to([P, NE])),
                (w_rt[:, :, 0:GROUPS], w_group[0].rearrange("(k p) n -> p k n", p=P)),
                (w_rt[:, :, GROUPS:NL], w_expert[0].rearrange("(k p) n -> p k n", p=P)),
            ]
            sp.dma_start(xt[:, :], x[0, 0:P, :]).then_inc(L.x_loaded, 16)
            for dst, src in small:
                sp.dma_start(dst, src, allow_slow_non_contiguous=True).then_inc(L.consts_loaded, 16)
            for c, (c0, n) in enumerate(CHUNKS):
                sp.dma_start(w_sb[:, :, c0:c0 + n],
                             w_in[0, :, c0:c0 + n].rearrange("(k p) n -> p k n", p=P)).then_inc(w_loaded[c], 16)
            sp.dma_start(wo_sb[:, :, :], w_out[0].rearrange("(k p) n -> p k n", p=P)).then_inc(wo_loaded, 16)

            def back(t):
                sp.wait_ge(B.p_turned, t + 1)
                sp.dma_start(xr[:, :], x[0, bass.ts(t, P), :]).then_inc(L.xr_loaded, 16)

            def store(t):
                sp.wait_ge(B.xm_ready, 2 * t + 2)
                sp.dma_start(x_mid[bass.ts(t, P), :], xr[:, :]).then_inc(L.mid_stored, 16)
                sp.wait_ge(B.hm_ready, t + 1)
                sp.dma_start(h_mid[bass.ts(t, P), :], y_mix[:, :]).then_inc(L.mid_stored, 16)

            def both(t):
                sp.wait_ge(F.h_turned, t + 1)
                sp.dma_start(xt[:, :], x[0, bass.ts(t + 1, P), :]).then_inc(L.x_loaded, 16)
                back(t)
                store(t)

            both(0)
            with sp.Fori(1, NT - 1) as i:
                both(i)
            back(NT - 1)
            store(NT - 1)
            sp.wait_ge(L.mid_stored, 32 * NT)

            def load_expert(m, b):
                if not isinstance(m, int) or m > 1:
                    sp.wait_ge(M.gu_done, m - 1)
                    sp.wait_ge(M.down_done, 2 * m - 2)
                e = sp.value_load(texp[0:1, bass.ds(m, 1)], min_val=0, max_val=NE - 1)
                sp.dma_start(wgu[b], w_gate_up[0, bass.ds(e, 1)].rearrange("o (k p) n -> p (o k) n", p=P)).then_inc(w1_loaded[b], 16)
                sp.dma_start(wdn[b], w_down[0, bass.ds(e, 1)].rearrange("o (k p) n -> p (o k) n", p=P)).then_inc(w2_loaded[b], 16)

            def store_y(m, b):
                sp.wait_ge(M.y0_ready, m + 1)
                sp.wait_ge(M.y1_ready, m + 1)
                sp.dma_start(y_slots[bass.ts(m, P), :], yo[b]).then_inc(y_stored[b], 16)

            sp.wait_ge(R.ready, 1)
            load_expert(0, 0)
            load_expert(1, 1)
            with sp.Fori(0, SLOT_TILES // 2 - 1) as u:
                load_expert(2 * u + 2, 0)
                store_y(2 * u, 0)
                load_expert(2 * u + 3, 1)
                store_y(2 * u + 1, 1)
            load_expert(SLOT_TILES - 1, 0)
            store_y(SLOT_TILES - 3, 0)
            store_y(SLOT_TILES - 2, 1)
            store_y(SLOT_TILES - 1, 0)
            for b in range(2):
                sp.wait_ge(y_stored[b], 16 * ((SLOT_TILES + 1 - b) // 2))
            for t in range(NT):
                if t > 1:
                    sp.wait_ge(out_stored[t % 2], 16 * (t // 2))
                sp.dma_start(out_x[t % 2], x_mid[t * P:(t + 1) * P, :]).then_inc(m_loaded[t % 2], 16)
                if t:
                    sp.wait_ge(M.summed, t)
                    sp.dma_start(out[0, (t - 1) * P:t * P, :], out_x[(t - 1) % 2]).then_inc(out_stored[(t - 1) % 2], 16)
            sp.wait_ge(M.summed, NT)
            sp.dma_start(out[0, (NT - 1) * P:, :], out_x[1]).then_inc(out_stored[1], 16)
            for b in range(2):
                sp.wait_ge(out_stored[b], 16 * NT // 2)

        @block.tensor
        def _(pe):
            def mm(o_, l_, r_, start=True, stop=True):
                return pe.matmul(o_, lhsT=l_, rhs=r_, start=start, stop=stop, skip_group_check=True)

            def turn(o_, in_):
                return pe.transpose(o_, in_, ident[:, :])

            def turn_h(t):
                pe.wait_ge(F.h_scaled, t + 1)
                if not isinstance(t, int) or t:
                    pe.wait_ge(F.ci_copied, 3 * t)
                for k in range(KD):
                    ins = turn(pm[k // 4][:, (k % 4) * P:(k % 4 + 1) * P], xt[:, k * P:(k + 1) * P])
                ins.then_inc(F.h_turned, 1)

            def project(t, c):
                c0, n = CHUNKS[c]
                if c < 2:
                    pe.wait_ge(F.hT_ready, 2 * t + 2)
                else:
                    pe.wait_ge(F.chunk_copied, 6 * t + c - 1)
                if isinstance(t, int) and t == 0:
                    pe.wait_ge(w_loaded[c], 16)
                for k in range(KD):
                    ins = mm(pm[c % 2][:, 0:n], hT[:, k, :], w_sb[:, k, c0:c0 + n], k == 0, k == KD - 1)
                ins.then_inc(F.chunk_done, 1)

            def turn_qkv(t, j):
                pe.wait_ge(F.chunk_copied, 6 * t + 5 + min(j, 1))
                if j == 2:
                    pe.wait_ge(F.ci_copied, 3 * t + 1)
                for h in range(H):
                    ins = turn(pm[j % 2][:, h * P:(h + 1) * P], pqkv[:, (H * j + h) * P:(H * j + h + 1) * P])
                ins.then_inc(F.turned, 1)

            def front(t):
                turn_h(t)
                for c in range(NC_):
                    project(t, c)
                for j in range(3):
                    turn_qkv(t, j)

            def both(t):
                back(t, t + 1)

            def back(t, nx=None):
                def ahead(c):
                    if nx is not None:
                        project(nx, c)

                pe.wait_ge(F.qkvT_ready, t + 1)
                if later(t):
                    pe.wait_ge(B.x_updated, 6 * t)
                    pe.wait_ge(B.v_ready, t)
                    pe.wait_ge(B.lg_ready, t)
                    pe.wait_ge(B.s_updated, t)
                for h in range(H):
                    turn(pm[2][:, h * P:(h + 1) * P], qkvT[:, H + h, :])
                for h in range(H):
                    ins = turn(pm[3][:, h * P:(h + 1) * P], qkvT[:, 2 * H + h, :])
                ins.then_inc(B.kv_turned, 1)
                pe.wait_ge(F.la_ready, t + 1)
                la = fs[:, 20:20 + H]
                for h in range(H):
                    ins = mm(pm[5][:, h * P:(h + 1) * P], la[:, h:h + 1].broadcast_to([P, P]), upper[:, :])
                ins.then_inc(B.gi_done, 1)
                mm(pm[4][:, 8:8 + H], upper[:, :], la)
                mm(pm[4][:, 12:12 + H], ones[:, :], la)
                pe.wait_ge(F.sq_ready, t + 1)
                for h in range(2 * H):
                    ins = mm(pm[4][:, h:h + 1], ctmp[:, h, :], ones[:, 0:1])
                ins.then_inc(B.small_done, 1)
                if nx is not None:
                    turn_h(nx)
                pe.wait_ge(F.qkn_ready, t + 1)
                if later(t):
                    pe.wait_ge(B.hT2_ready, 2 * t)
                for g in range(GRP):
                    turn(pm[6][:, g * P:(g + 1) * P],
                         qkn[:, KVH * g:KVH * g + KVH, :].rearrange("p h d -> p (h d)"))
                turn(pm[7][:, 0:P], qkn[:, QH:QH + KVH, :].rearrange("p h d -> p (h d)")).then_inc(B.swa_turned, 1)
                pe.wait_ge(B.kn_ready, t + 1)
                for h in range(H):
                    ins = turn(pm[2][:, h * P:(h + 1) * P], kn[:, h, :])
                ins.then_inc(B.kn_turned, 1)
                ahead(0)
                pe.wait_ge(B.knT_ready, t + 1)
                pe.wait_ge(B.vt_ready, t + 1)
                for h in range(H):
                    ins = mm(pm[3][:, h * P:(h + 1) * P], knT[:, h, :], knT[:, h, :])
                ins.then_inc(B.kk_done, 1)
                pe.wait_ge(B.qT_ready, t + 1)
                pe.wait_ge(B.kWin_ready, t + 1)
                pe.wait_ge(B.diff_ready, t + 1)
                for h in range(H):
                    ins = mm(pm[5][:, h * P:(h + 1) * P], knT[:, h, :], qkvT[:, h, :])
                ins.then_inc(B.qk_done, 1)
                for kv in range(KVH):
                    for half in range(2):
                        keys = kWin[kv * DH:(kv + 1) * DH, 0:3:1 + half, :]
                        if half == 0:
                            keys = kWin[kv * DH:(kv + 1) * DH, 0:2, :]
                        for g in range(GRP):
                            ins = mm(pm[6 + kv][half * CH:(half + 1) * CH, g * P:(g + 1) * P],
                                     qT[kv * DH:(kv + 1) * DH, g, half * CH:(half + 1) * CH], keys)
                ins.then_inc(B.scores_done, 1)
                pe.wait_ge(B.xT0_ready, t + 1)
                for h in range(H):
                    ins = turn(pm[2][:, h * P:(h + 1) * P], XT[:, h, :])
                ins.then_inc(B.x0_turned, 1)
                ahead(1)
                pe.wait_ge(B.x0_copied, t + 1)
                n = len(LEVELS)
                for l in range(n):
                    pe.wait_ge(B.aTm_ready, 6 * t + l + 1)
                    if l:
                        pe.wait_ge(B.x_updated, 6 * t + l)
                    else:
                        pe.wait_ge(B.aT_ready, t + 1)
                    for h in range(H):
                        ins = mm(pm[3][:, h * P:(h + 1) * P], aTm[:, l % 2, h, :], X[:, h, :])
                    ins.then_inc(B.y_done, 1)
                    if l == 0:
                        if later(t):
                            pe.wait_ge(B.s_updated, t)
                        for h in range(H):
                            ins = mm(pm[4][:, h * P:(h + 1) * P], knT[:, h, :], S[:, h, :])
                        ins.then_inc(B.ks_done, 1)
                    elif l in (1, 3):
                        ahead(2 + l // 2)
                    elif l == 2:
                        pe.wait_ge(B.p_ready, t + 1)
                        for h in range(QH):
                            ins = turn(pm[6 + h // 4][:, (h % 4) * P:(h % 4 + 1) * P], sc[:, h, :])
                        ins.then_inc(B.p_turned, 1)
                    elif l == 4:
                        pe.wait_ge(B.pT_ready, t + 1)
                        pe.wait_ge(B.vWin_ready, t + 1)
                        for half in range(2):
                            for h in range(QH):
                                kv, g = h // GRP, h % GRP
                                ins = mm(pm[6 + kv][half * CH:(half + 1) * CH, g * (DH + 1):(g + 1) * (DH + 1)],
                                         pT[:, h, half * CH:(half + 1) * CH], vWin[:, half, kv, :])
                        ins.then_inc(B.pv_done, 1)
                    pe.wait_ge(B.y_copied, 6 * t + l + 1)
                    if l == 0:
                        pe.wait_ge(B.qkT_ready, t + 1)
                    for h in range(H):
                        mm(pm[5][:, h * P:(h + 1) * P], Y[:, h, :], XT[:, h, :])
                    if l < n - 1:
                        for h in range(H):
                            ins = mm(pm[2][:, h * P:(h + 1) * P], XT[:, h, :], Y[:, h, :])
                    else:
                        for h in range(H):
                            ins = mm(pm[2][:, h * P:(h + 1) * P], qkvT[:, h, :], S[:, h, :])
                    ins.then_inc(B.z_done, 1)
                ahead(4)
                pe.wait_ge(B.x_updated, 6 * t + 6)
                pe.wait_ge(B.r_ready, t + 1)
                for h in range(H):
                    ins = mm(pm[3][:, h * P:(h + 1) * P], XT[:, h, :], r[:, h, :])
                ins.then_inc(B.v0_done, 1)
                ahead(5)
                pe.wait_ge(B.v_ready, t + 1)
                pe.wait_ge(B.kd_ready, t + 1)
                for h in range(H):
                    ins = mm(pm[5][:, h * P:(h + 1) * P], kd[:, h, :], V[:, h, :])
                ins.then_inc(B.s_done, 1)
                for h in range(H):
                    ins = mm(pm[4][:, h * P:(h + 1) * P], qkT[:, h, :], V[:, h, :])
                ins.then_inc(B.o2_done, 1)
                if nx is not None:
                    for j in range(3):
                        turn_qkv(nx, j)
                pe.wait_ge(B.ya_ready, t + 1)
                pe.wait_ge(B.yb_ready, t + 1)
                for k in range(KD):
                    ins = turn(pm[6 + k // 4][:, (k % 4) * P:(k % 4 + 1) * P], y_mix[:, k * P:(k + 1) * P])
                ins.then_inc(B.y_turned, 1)
                pe.wait_ge(B.yT_ready, t + 1)
                if isinstance(t, int) and t == 0:
                    pe.wait_ge(wo_loaded, 16)
                for n_ in range(2):
                    for k in range(KD):
                        ins = mm(pm[6 + n_][:, :], yT[:, k, :], wo_sb[:, k, n_ * 512:(n_ + 1) * 512],
                                 k == 0, k == KD - 1)
                    ins.then_inc(B.out_done, 1)
                pe.wait_ge(B.hm_ready, t + 1)
                for k in range(KD):
                    ins = turn(pm[6 + k // 4][:, (k % 4) * P:(k % 4 + 1) * P], y_mix[:, k * P:(k + 1) * P])
                ins.then_inc(B.hm_turned, 1)
                pe.wait_ge(B.hT2_ready, 2 * t + 2)
                pe.wait_ge(B.o_ready, t + 1)
                for k in range(KD):
                    ins = mm(pm[4][:, 0:NL], hT2[:, k, :], w_rt[:, k, :], k == 0, k == KD - 1)
                ins.then_inc(B.logits_done, 1)

            pe.wait_ge(L.masks_made, 1)
            pe.wait_ge(L.consts_loaded, 16 * NSMALL)
            run_tiles(pe, front, both, back)

            pe.wait_ge(R.picks, 1)
            picks = both_picks.rearrange("p t g e -> p (t g e)")
            mm(pm[0][:, 0:P], upper_strict[:, :], picks)
            mm(pm[0][:, P:2 * P], ones[:, :], picks).then_inc(R.counts, 1)
            pe.wait_ge(R.hots, 1)
            for u in range(TOPK * NT):
                ins = mm(pm[1][:, 0:32], hot_mod[u], hot_div[:, u, :], u == 0, u == TOPK * NT - 1)
            ins.then_inc(R.idx_summed, 1)

            def turn_rows(m, b, u):
                pe.wait_ge(gathered[b], 16 * u + 16)
                if later(m):
                    pe.wait_ge(M.hT_ready, 2 * m)
                for k in range(KD):
                    ins = turn(pm[k // 4][:, (k % 4) * P:(k % 4 + 1) * P], hg[b][:, k * P:(k + 1) * P])
                ins.then_inc(M.turned, 1)

            def gate_up(m, b, u):
                pe.wait_ge(M.hT_ready, 2 * m + 2)
                pe.wait_ge(w1_loaded[b], 16 * u + 16)
                for k in range(KD):
                    ins = mm(pm[2 + b][:, :], hgT[b][:, k, :], wgu[b][:, k, :], k == 0, k == KD - 1)
                ins.then_inc(M.gu_done, 1)

            def down(m, b, u):
                pe.wait_ge(M.glu_ready, m + 1)
                for k in range(DE // P):
                    ins = turn(pm[4][:, k * P:(k + 1) * P], glu[:, k * P:(k + 1) * P])
                ins.then_inc(M.glu_turned, 1)
                pe.wait_ge(w2_loaded[b], 16 * u + 16)
                if later(m):
                    pe.wait_ge(M.y0_ready, m)
                    pe.wait_ge(M.y1_ready, m)
                pe.wait_ge(M.gluT_ready, m + 1)
                for n in range(2):
                    for k in range(DE // P):
                        ins = mm(pm[6 + n][:, :], gluT[:, k, :], wdn[b][:, k, n * 512:(n + 1) * 512], k == 0,
                                 k == DE // P - 1)
                    ins.then_inc(M.down_done, 1)

            def step(m, b, u):
                if not isinstance(m, int) or m < SLOT_TILES - 1:
                    turn_rows(m + 1, 1 - b, u + b)
                gate_up(m, b, u)
                if later(m):
                    down(m - 1, 1 - b, u - 1 + b)

            turn_rows(0, 0, 0)
            run_slots(pe, step, lambda: down(SLOT_TILES - 1, 0, SLOT_TILES // 2))

        @block.scalar
        def _(act):
            def square_x(t):
                act.wait_ge(L.x_loaded, 16 * t + 16)
                act.activation(hT[:, :, :], xt[:, :].rearrange("p (k n) -> p k n", n=P), ACT.Square, accum_out=fs[:, 0:1]).then_inc(F.ssx_ready, 1)

            def copy_chunk(t, c):
                c0, n = CHUNKS[c]
                act.wait_ge(F.chunk_done, 6 * t + c + 1)
                dst = pqkv[:, c0:c0 + n] if c < 3 else tail[:, c0 - 3 * HP:c0 - 3 * HP + n]
                if c == 3 and later(t):
                    act.wait_ge(F.gsz_ready, t)
                    act.wait_ge(F.qkn_ready, t)
                    act.wait_ge(F.la_ready, t)
                    act.wait_ge(B.vWin_ready, t)
                act.activation(dst, pm[c % 2][:, 0:n], ACT.Copy).then_inc(F.chunk_copied, 1)

            def copy_ci(t, j):
                act.wait_ge(F.turned, 3 * t + j + 1)
                if j == 0:
                    act.wait_ge(F.halo_ready, t + 1)
                act.activation(ci[:, H * j:H * j + H, HALO:HALO + P], heads(pm[j % 2]), ACT.Copy).then_inc(F.ci_copied, 1)

            def gates(t):
                act.wait_ge(F.u_ready, t + 1)
                act.activation(fs[:, 12:12 + H], fs[:, 8:8 + H], ACT.Exp).then_inc(F.exp_ready, 1)
                act.wait_ge(F.exp_ready, t + 1)
                act.activation(fs[:, 16:16 + H], fs[:, 12:12 + H], ACT.Ln, bias=1.0).then_inc(F.ln_ready, 1)
                act.activation(fs[:, 24:24 + H], tail[:, BE0:BE0 + H], ACT.Tanh, scale=0.5)
                act.activation(gsz[:, :, :], tail[:, Z0:Z0 + HP].rearrange("p (h n) -> p h n", h=H), ACT.Tanh,
                               scale=0.5).then_inc(F.tz_ready, 1)

            def silu(t):
                act.wait_ge(F.conv_done, t + 1)
                act.activation(ctmp[:, :, :], cv[:, :, :], ACT.Tanh).then_inc(F.tanh_ready, 1)

            def front(t):
                square_x(t)
                for c in range(NC_):
                    copy_chunk(t, c)
                gates(t)
                for j in range(3):
                    copy_ci(t, j)
                silu(t)

            def both(t):
                back(t, t + 1)

            def back(t, nx=None):
                def ahead(c):
                    if nx is not None:
                        copy_chunk(nx, c)

                act.wait_ge(B.kv_turned, t + 1)
                act.activation(vt[:, :, :], heads(pm[3]), ACT.Copy).then_inc(B.vt_ready, 1)
                act.wait_ge(B.diff_ready, t + 1)
                act.activation(dT[:, :, :], dT[:, :, :], ACT.Exp).then_inc(B.dT_exp, 1)
                act.activation(bs[:, 0:3 * H], bs[:, 12:12 + 3 * H], ACT.Exp).then_inc(B.eg_ready, 1)
                if nx is not None:
                    square_x(nx)
                act.wait_ge(B.swa_turned, t + 1)
                act.activation(qT[:, :, :], heads(pm[6]), ACT.Copy).then_inc(B.qT_ready, 1)
                act.wait_ge(B.kOld_ready, t + 1)
                act.activation(kWin[:, 0:3:2, :], pm[7][:, 0:P].rearrange("p (a b) -> p a b", a=2),
                               ACT.Copy).then_inc(B.kWin_ready, 1)
                act.wait_ge(B.kn_turned, t + 1)
                act.activation(knT[:, :, :], heads(pm[2]), ACT.Copy).then_inc(B.knT_ready, 1)
                ahead(0)
                act.wait_ge(B.x0_turned, t + 1)
                act.activation(X[:, :, :], heads(pm[2]), ACT.Copy).then_inc(B.x0_copied, 1)
                ahead(1)
                for l in range(len(LEVELS)):
                    act.wait_ge(B.y_done, 6 * t + l + 1)
                    act.activation(Y[:, :, :], heads(pm[3]), ACT.Copy).then_inc(B.y_copied, 1)
                    if l == 1:
                        ahead(2)
                        act.wait_ge(B.sc_ready, t + 1)
                        act.activation(sc[:, :, :], sc[:, :, :], ACT.Exp, scale=DH ** -0.5).then_inc(B.p_ready, 1)
                        act.activation(bs[:, 56:64], bs[:, 48:56], ACT.Exp, scale=DH ** -0.5).then_inc(B.sink_exp, 1)
                    if l == 3:
                        ahead(3)
                        act.wait_ge(B.p_turned, t + 1)
                        act.activation(pT[:, 0:4, :], heads(pm[6]), ACT.Copy)
                        act.activation(pT[:, 4:8, :], heads(pm[7]), ACT.Copy).then_inc(B.pT_ready, 1)
                ahead(4)
                ahead(5)
                if nx is not None:
                    for j in range(3):
                        copy_ci(nx, j)
                act.wait_ge(B.y_turned, t + 1)
                act.activation(yT[:, 0:4, :], heads(pm[6]), ACT.Copy)
                act.activation(yT[:, 4:8, :], heads(pm[7]), ACT.Copy).then_inc(B.yT_ready, 1)
                if nx is not None:
                    gates(nx)
                    silu(nx)
                act.wait_ge(B.xm_ready, 2 * t + 2)
                act.activation(y_mix[:, :], xr[:, :], ACT.Square, accum_out=bs[:, 88:89]).then_inc(B.ss2_ready, 1)

            act.wait_ge(L.consts_loaded, 16 * NSMALL)
            act.activation(neg_a, neg_a, ACT.Exp).then_inc(L.weights_ready, 1)
            run_tiles(act, front, both, back)
            act.wait_ge(R.exp_in, 1)
            act.activation(ex, ex, ACT.Exp).then_inc(R.exp_out, 1)

            def step(m, b, u):
                act.wait_ge(M.gu_done, m + 1)
                if later(m):
                    act.wait_ge(M.glu_ready, m)
                act.activation(tnh, pm[2 + b][:, 0:DE], ACT.Tanh, scale=0.5).then_inc(M.tanh_ready, 1)
                if later(m):
                    copy_out(m - 1, 1 - b, u - 1 + b)

            def copy_out(m, b, u):
                act.wait_ge(M.down_done, 2 * m + 2)
                if not isinstance(u, int) or u > 0:
                    act.wait_ge(y_stored[b], 16 * u)
                act.activation(yo[b][:, 512:], pm[7][:, :], ACT.Copy).then_inc(M.y1_ready, 1)

            run_slots(act, step, lambda: copy_out(SLOT_TILES - 1, 0, SLOT_TILES // 2))

        @block.vector
        def _(v):
            def stepper(sem, t, per):
                count = [0]

                def step(ins):
                    count[0] += 1
                    ins.then_inc(sem, 1)
                    v.wait_ge(sem, per * t + count[0])
                return step, count

            def rsqrt(step, y, a, tmp, src, scale):
                step(v.tensor_scalar(a, src, scale, EPS, ALU.mult, ALU.add))
                step(v.tensor_scalar(y.bitcast(I32), a.bitcast(I32), 1, None, ALU.logical_shift_right))
                step(v.tensor_scalar(y.bitcast(I32), y.bitcast(I32), -1, RSQRT_MAGIC, ALU.mult, ALU.add))
                for _i in range(3):
                    step(v.tensor_tensor(tmp, y, y, ALU.mult))
                    step(v.scalar_tensor_tensor(tmp, tmp, -0.5, a, ALU.mult, ALU.mult))
                    step(v.scalar_tensor_tensor(y, tmp, 1.5, y, ALU.add, ALU.mult))

            class Front:

                def __init__(self, t):
                    self.t = t
                    self.step, self.count = stepper(F.front_step, t, VF)

                def scale_x(self):
                    v.wait_ge(F.ssx_ready, self.t + 1)
                    rsqrt(self.step, fs[:, 1:2], fs[:, 2:3], fs[:, 3:4], fs[:, 0:1], 1.0 / D)
                    v.tensor_scalar(xt[:, :], xt[:, :], fs[:, 1:2], None, ALU.mult).then_inc(F.h_scaled, 1)

                def copy_hT(self):
                    v.wait_ge(F.h_turned, self.t + 1)
                    for b in range(2):
                        v.tensor_tensor(hT[:, 4 * b:4 * b + 4, :], heads(pm[b]), wide(gain1[:, 4 * b:4 * b + 4]),
                                        ALU.mult).then_inc(F.hT_ready, 1)

                def gate_inputs(self):
                    v.wait_ge(F.chunk_copied, 6 * self.t + 5)
                    self.step(v.tensor_tensor(fs[:, 4:8], tail[:, AL0:AL0 + H], dtb, ALU.add))
                    self.step(v.tensor_scalar(fs[:, 12:16], fs[:, 4:8], 0.0, None, ALU.max))
                    v.scalar_tensor_tensor(fs[:, 8:12], fs[:, 12:16], -2.0, fs[:, 4:8], ALU.mult,
                                           ALU.add).then_inc(F.u_ready, 1)

                def conv(self):
                    v.wait_ge(F.ci_copied, 3 * self.t + 3)
                    self.step(v.tensor_tensor(cv[:, :, :], ci[:, :, 0:P], wide(cw[:, 0, :]), ALU.mult))
                    for j in range(1, KW):
                        self.step(v.tensor_tensor(ctmp[:, :, :], ci[:, :, j:j + P], wide(cw[:, j, :]), ALU.mult))
                        ins = v.tensor_tensor(cv[:, :, :], cv[:, :, :], ctmp[:, :, :], ALU.add)
                        if j < KW - 1:
                            self.step(ins)
                    ins.then_inc(F.conv_done, 1)

                def gate_outputs(self):
                    v.wait_ge(F.ln_ready, self.t + 1)
                    self.step(v.tensor_scalar(fs[:, 4:8], fs[:, 4:8], 0.0, None, ALU.max))
                    self.step(v.tensor_tensor(fs[:, 16:20], fs[:, 16:20], fs[:, 4:8], ALU.add))
                    v.wait_ge(F.tz_ready, self.t + 1)
                    v.tensor_tensor(fs[:, 20:24], fs[:, 16:20], neg_a, ALU.mult)
                    v.tensor_scalar(fs[:, 28:32], fs[:, 24:28], 0.5, 0.5, ALU.mult, ALU.add).then_inc(F.la_ready, 1)
                    v.wait_ge(F.hz_ready, self.t + 1)
                    v.scalar_tensor_tensor(gsz[:, :, :], gsz[:, :, :], 1.0,
                                           tail[:, Z0:Z0 + HP].rearrange("p (h n) -> p h n", h=H),
                                           ALU.add, ALU.mult).then_inc(F.gsz_ready, 1)

                def attention_norm(self):
                    v.wait_ge(F.swa_squared, self.t + 1)
                    self.step(v.tensor_reduce(fs[:, 32:42], qkg[:, :, :], AX_X, ALU.add))
                    rsqrt(self.step, fs[:, 42:52], fs[:, 52:62], fs[:, 62:72], fs[:, 32:42], 1.0 / DH)
                    v.wait_ge(F.swa_gained, self.t + 1)
                    v.tensor_tensor(qkn[:, 0:QH, :].rearrange("p (g kv) n -> p kv g n", kv=KVH),
                                    tail[:, SQ0:SK0].rearrange("p (kv g n) -> p kv g n", kv=KVH, g=GRP),
                                    fs[:, 42:42 + QH].rearrange("p (kv g) -> p kv g", kv=KVH).unsqueeze(3)
                                    .broadcast_to([P, KVH, GRP, DH]), ALU.mult)
                    v.tensor_tensor(qkn[:, QH:, :], tail[:, SK0:SV0].rearrange("p (h n) -> p h n", n=DH),
                                    wide(fs[:, 42 + QH:52], DH), ALU.mult).then_inc(F.qkn_ready, 1)

                def silu(self):
                    v.wait_ge(F.tanh_ready, self.t + 1)
                    v.scalar_tensor_tensor(qkvT[:, :, :], ctmp[:, :, :], 1.0, cv[:, :, :], ALU.add,
                                           ALU.mult).then_inc(F.qkvT_ready, 1)

            def front(t):
                f = Front(t)
                f.scale_x()
                f.copy_hT()
                f.gate_inputs()
                f.conv()
                f.gate_outputs()
                f.attention_norm()
                f.silu()

            def both(t):
                back(t, Front(t + 1))

            def back(t, nx=None):
                step, count = stepper(B.back_step, t, VB)
                eg, ekl, cd = bs[:, 0:4], bs[:, 4:8], bs[:, 8:12]
                beta = fs[:, 28:32]
                v.wait_ge(B.small_done, t + 1)
                if later(t):
                    v.wait_ge(B.eg_ready, t)
                step(v.tensor_copy(bs[:, 12:16], pm[4][:, 8:12]))
                v.tensor_copy(bs[:, 20:24], pm[4][:, 12:16])
                v.tensor_tensor(bs[:, 16:20], pm[4][:, 12:16], bs[:, 12:16], ALU.subtract)
                step(v.tensor_tensor(dT[:, :, :], heads(pm[5]), wide(bs[:, 12:16]), ALU.subtract))
                v.tensor_scalar(dT[:, :, :], dT[:, :, :], 0.0, None, ALU.min).then_inc(B.diff_ready, 1)
                rsqrt(step, bs[:, 24:32], bs[:, 32:40], bs[:, 40:48], pm[4][:, 0:8], 1.0)
                v.tensor_tensor(kn[:, :, :], heads(pm[2]), wide(bs[:, 28:32]), ALU.mult).then_inc(B.kn_ready, 1)
                if nx:
                    nx.scale_x()
                    nx.copy_hT()
                v.wait_ge(B.dT_exp, t + 1)
                step(v.tensor_tensor(dT[:, :, :], dT[:, :, :], upper[:, None, :].broadcast_to([P, H, P]), ALU.mult))
                v.wait_ge(B.kk_done, t + 1)
                step(v.tensor_tensor(aT[:, :, :], heads(pm[3]), dT[:, :, :], ALU.mult))
                v.tensor_tensor(aT[:, :, :], aT[:, :, :], wide(beta), ALU.mult).then_inc(B.aT_ready, 1)
                v.wait_ge(B.aT_ready, t + 1)
                step(v.tensor_tensor(XT[:, :, :], aT[:, :, :], level_mask[:, 0:1, :].broadcast_to([P, H, P]),
                                     ALU.mult))
                v.tensor_tensor(XT[:, :, :], ident[:, None, :].broadcast_to([P, H, P]), XT[:, :, :],
                                ALU.subtract).then_inc(B.xT0_ready, 1)
                v.wait_ge(B.qk_done, t + 1)
                v.tensor_tensor(qkT[:, :, :], heads(pm[5]), dT[:, :, :], ALU.mult).then_inc(B.qkT_ready, 1)
                for l in range(len(LEVELS)):
                    v.wait_ge(B.z_done, 6 * t + l + 1)
                    if l < len(LEVELS) - 1:
                        v.tensor_tensor(X[:, :, :], X[:, :, :], heads(pm[2]), ALU.subtract)
                    else:
                        v.tensor_tensor(o[:, :, :], heads(pm[2]), wide(eg), ALU.mult)
                    v.tensor_tensor(XT[:, :, :], XT[:, :, :], heads(pm[5]), ALU.subtract).then_inc(B.x_updated, 1)
                    if l == 0:
                        v.wait_ge(B.scores_done, t + 1)
                        if later(t):
                            v.wait_ge(L.mid_stored, 32 * t)
                        top = bs[:, 64:72]
                        for kv in range(KVH):
                            src = heads(pm[6 + kv])
                            if not later(t):
                                v.tensor_tensor(sc[:, 4 * kv:4 * kv + 4, :], src,
                                                key_mask[:, None, :].broadcast_to([P, GRP, P]),
                                                ALU.add).then_inc(L.masked, 1)
                                v.wait_ge(L.masked, kv + 1)
                                src = sc[:, 4 * kv:4 * kv + 4, :]
                            ins = v.tensor_reduce(top[:, 4 * kv:4 * kv + 4], src, AX_X, ALU.max)
                        ins.then_inc(B.top_found, 1)
                        v.wait_ge(B.top_found, t + 1)
                        step(v.tensor_tensor(top, top, sink, ALU.max))
                        for kv in range(KVH):
                            src = sc[:, 4 * kv:4 * kv + 4, :] if not later(t) else heads(pm[6 + kv])
                            v.tensor_tensor(sc[:, 4 * kv:4 * kv + 4, :], src, wide(top[:, 4 * kv:4 * kv + 4]),
                                            ALU.subtract)
                        v.tensor_tensor(bs[:, 48:56], sink, top, ALU.subtract).then_inc(B.sc_ready, 1)
                    if l == 2:
                        v.wait_ge(B.ks_done, t + 1)
                        v.wait_ge(B.eg_ready, t + 1)
                        v.wait_ge(B.vt_ready, t + 1)
                        step(v.tensor_tensor(V[:, :, :], heads(pm[4]), wide(eg), ALU.mult))
                        v.tensor_tensor(r[:, :, :], vt[:, :, :], V[:, :, :], ALU.subtract).then_inc(B.r_ready, 1)
                v.wait_ge(B.v0_done, t + 1)
                v.tensor_tensor(V[:, :, :], heads(pm[3]), wide(beta), ALU.mult).then_inc(B.v_ready, 1)
                step(v.tensor_tensor(S[:, :, :], S[:, :, :], wide(cd), ALU.mult))
                v.wait_ge(B.pv_done, t + 1)
                v.wait_ge(B.sink_exp, t + 1)
                if later(t):
                    v.wait_ge(L.mid_stored, 32 * t)
                pv = [pm[6 + kv][:, 0:GRP * (DH + 1)].rearrange("p (g n) -> p g n", n=DH + 1) for kv in range(KVH)]
                for kv in range(KVH):
                    ins = v.tensor_tensor(bs[:, 96 + 4 * kv:100 + 4 * kv], pv[kv][:, :, DH], bs[:, 56 + 4 * kv:60 + 4 * kv],
                                          ALU.add)
                step(ins)
                step(v.reciprocal(bs[:, 104:112], bs[:, 96:104]))
                for kv in range(KVH):
                    ins = v.tensor_tensor(
                        y_mix[:, HP + 256 * kv:HP + 256 * kv + 256].rearrange("p (g n) -> p g n", n=DH),
                        pv[kv][:, :, 0:DH], wide(bs[:, 104 + 4 * kv:108 + 4 * kv], DH), ALU.mult)
                ins.then_inc(B.yb_ready, 1)
                v.wait_ge(B.s_done, t + 1)
                v.tensor_tensor(S[:, :, :], S[:, :, :], heads(pm[5]), ALU.add).then_inc(B.s_updated, 1)
                v.wait_ge(B.o2_done, t + 1)
                step(v.tensor_tensor(o[:, :, :], o[:, :, :], heads(pm[4]), ALU.add))
                v.scalar_tensor_tensor(o[:, :, :], o[:, :, :], float(P) ** -0.5, wide(bs[:, 24:28]), ALU.mult,
                                       ALU.mult).then_inc(B.o_ready, 1)
                v.wait_ge(B.o_squared, t + 1)
                step(v.tensor_reduce(bs[:, 72:76], o2[:, :, :], AX_X, ALU.add))
                rsqrt(step, bs[:, 76:80], bs[:, 80:84], bs[:, 84:88], bs[:, 72:76], 1.0 / P)
                step(v.tensor_tensor(o[:, :, :], o[:, :, :], wide(bs[:, 76:80]), ALU.mult))
                v.tensor_tensor(y_mix[:, 0:HP].rearrange("p (h n) -> p h n", h=H), o[:, :, :], gsz[:, :, :],
                                ALU.mult).then_inc(B.ya_ready, 1)
                if nx:
                    nx.gate_inputs()
                    nx.conv()
                v.wait_ge(L.xr_loaded, 16 * t + 16)
                for n_ in range(2):
                    v.wait_ge(B.out_done, 2 * t + n_ + 1)
                    v.tensor_tensor(xr[:, 512 * n_:512 * n_ + 512], xr[:, 512 * n_:512 * n_ + 512], pm[6 + n_][:, :],
                                    ALU.add).then_inc(B.xm_ready, 1)
                if nx:
                    nx.gate_outputs()
                v.wait_ge(B.ss2_ready, t + 1)
                rsqrt(step, bs[:, 89:90], bs[:, 90:91], bs[:, 91:92], bs[:, 88:89], 1.0 / D)
                v.tensor_scalar(y_mix[:, :], xr[:, :], bs[:, 89:90], None, ALU.mult).then_inc(B.hm_ready, 1)
                if nx:
                    nx.silu()
                v.wait_ge(B.hm_turned, t + 1)
                for b in range(2):
                    v.tensor_tensor(hT2[:, 4 * b:4 * b + 4, :], heads(pm[6 + b]), wide(gain2[:, 4 * b:4 * b + 4]),
                                    ALU.mult).then_inc(B.hT2_ready, 1)
                if nx:
                    nx.attention_norm()
                    assert nx.count[0] == VF, nx.count
                v.wait_ge(B.logits_done, t + 1)
                v.tensor_tensor(lg[:, bass.ds(t, 1), :], pm[4][:, 0:NL].unsqueeze(1), b_rt.unsqueeze(1), ALU.add).then_inc(B.lg_ready, 1)
                assert count[0] == VB, count

            v.wait_ge(L.consts_loaded, 16 * NSMALL)
            v.wait_ge(L.weights_ready, 1)
            v.tensor_scalar(neg_a, neg_a, -1.0, None, ALU.mult)
            v.tensor_scalar(g_out, g_out, 0.5, None, ALU.mult)
            v.tensor_scalar(sink, sink, DH ** 0.5, None, ALU.mult)
            v.tensor_scalar(cw[:, :, :], cw[:, :, :], 0.5, None, ALU.mult).then_inc(L.dve_consts, 1)
            v.wait_ge(L.dve_consts, 1)
            v.wait_ge(L.masks_made, 1)
            run_tiles(v, front, both, back)
            v.wait_ge(B.lg_ready, NT)
            v.wait_ge(R.iotas, 1)
            step, count = stepper(R.route_step, 0, 0)

            def tt(dst, a, b, op):
                step(v.tensor_tensor(dst, a, b, op))

            def over_last(ap2, n):
                return ap2.unsqueeze(len(ap2.shape)).broadcast_to(list(ap2.shape) + [n])

            def first_only(hot):
                step(v.tensor_copy(seen, hot[:, :, 0]))
                for i in range(1, hot.shape[2]):
                    tt(hot[:, :, i], hot[:, :, i], seen, ALU.is_gt)
                    tt(seen, seen, hot[:, :, i], ALU.max)

            gl, el = lg[:, :, 0:GROUPS], lg[:, :, GROUPS:NL].rearrange("p t (g e) -> p t g e", g=GROUPS)
            step(v.tensor_reduce(gmax, gl, AX_X, ALU.max))
            tt(ex[:, 0:NT * GROUPS].rearrange("p (t g) -> p t g", g=GROUPS), gl, over_last(gmax, GROUPS), ALU.subtract)
            tt(og, gl, over_last(gmax, GROUPS), ALU.is_equal)
            first_only(og)
            tt(prod, el, over_last(og, EPG), ALU.mult)
            step(v.tensor_reduce(es, prod.rearrange("p t g e -> p t e g"), AX_X, ALU.add))
            step(v.tensor_reduce(m1, es, AX_X, ALU.max))
            tt(e1, es, over_last(m1, EPG), ALU.is_equal)
            first_only(e1)
            step(v.scalar_tensor_tensor(es, e1, -BIG, es, ALU.mult, ALU.add))
            step(v.tensor_reduce(m2, es, AX_X, ALU.max))
            tt(e2, es, over_last(m2, EPG), ALU.is_equal)
            first_only(e2)
            v.tensor_tensor(ex[:, NT * GROUPS:], m2, m1, ALU.subtract).then_inc(R.exp_in, 1)
            for pick, e in ((pick1, e1), (pick2, e2)):
                tt(pick, over_last(og, EPG), e.unsqueeze(2).broadcast_to([P, NT, GROUPS, EPG]), ALU.mult)
            v.tensor_tensor(both_picks, pick1, pick2, ALU.add).then_inc(R.picks, 1)
            v.wait_ge(R.exp_out, 1)
            step(v.tensor_reduce(sump, ex[:, 0:NT * GROUPS].rearrange("p (t g) -> p t g", g=GROUPS), AX_X, ALU.add))
            step(v.scalar_tensor_tensor(sump, ex[:, NT * GROUPS:], 1.0, sump, ALU.add, ALU.mult))
            step(v.reciprocal(gate1, sump))
            tt(gate2, gate1, ex[:, NT * GROUPS:], ALU.mult)
            v.wait_ge(R.counts, 1)
            step(v.memset(run[:, 0, :], 0.0))
            tot = pm[0][:, P:2 * P].rearrange("p (t e) -> p t e", e=NE)
            for t in range(NT):
                tt(run[:, t + 1, :], tot[:, t, :], run[:, t, :], ALU.add)
            tt(slot, pm[0][:, 0:P].rearrange("p (t e) -> p t e", e=NE), run[:, 0:NT, :], ALU.add)
            tt(over, over_last(run[:, NT, :], NT), step_f.unsqueeze(1).broadcast_to([P, NE, NT]), ALU.is_gt)
            step(v.tensor_reduce(tiles_of, over, AX_X, ALU.add))
            step(v.tensor_tensor_scan(tiles_to, ones[:, 0:NE], tiles_of, 0.0, ALU.mult, ALU.add))
            tt(base, tiles_to, tiles_of, ALU.subtract)
            step(v.scalar_tensor_tensor(slot, base.unsqueeze(1).broadcast_to([P, NT, NE]), float(P), slot,
                                        ALU.mult, ALU.add))
            for c, pick in enumerate((pick1, pick2)):
                tt(prod, pick, slot.rearrange("p t (g e) -> p t g e", g=GROUPS), ALU.mult)
                step(v.tensor_reduce(slots[:, c * NT:(c + 1) * NT], prod.rearrange("p t g e -> p t (g e)"), AX_X, ALU.add))
            tt(past[0:1], tiles_to[0:1].unsqueeze(1).broadcast_to([1, SLOT_TILES + 1, NE]),
               over_last(iota_f[0:1, 0:SLOT_TILES + 1], NE), ALU.is_le)
            step(v.tensor_reduce(texp_f[0:1], past[0:1], AX_X, ALU.add))
            step(v.tensor_scalar(texp_f[0:1], texp_f[0:1], float(NE - 1), None, ALU.min))
            step(v.tensor_copy(texp[0:1], texp_f[0:1]))
            step(v.tensor_copy(slots_i, slots))
            step(v.tensor_scalar(mod_i, slots_i, P - 1, None, ALU.bitwise_and))
            step(v.tensor_scalar(div_i, slots_i, P.bit_length() - 1, None, ALU.logical_shift_right))
            step(v.tensor_copy(mod_f, mod_i))
            v.tensor_copy(div_f, div_i).then_inc(R.ready, 1)
            v.wait_ge(R.ready, 1)
            for u in range(TOPK * NT):
                v.tensor_scalar(hot_mod[u], iota_f, mod_f[:, u:u + 1], tok_f[:, u % NT:u % NT + 1], ALU.is_equal, ALU.mult)
                ins = v.tensor_scalar(hot_div[:, u, :], iota_f[:, 0:32], div_f[:, u:u + 1], None, ALU.is_equal)
            ins.then_inc(R.hots, 1)
            v.wait_ge(R.idx_summed, 1)
            v.tensor_copy(idx, pm[1][:, 0:32]).then_inc(R.idx_ready, 1)

            def copy_rows(m, b, u):
                v.wait_ge(M.turned, m + 1)
                for n in range(2):
                    if n == 0 and (not isinstance(m, int) or m > 1):
                        v.wait_ge(M.gu_done, m - 1)
                    v.tensor_tensor(hgT[b][:, 4 * n:4 * n + 4, :], heads(pm[n]), wide(gain2[:, 4 * n:4 * n + 4]),
                                    ALU.mult).then_inc(M.hT_ready, 1)

            def swiglu(m, b, u):
                v.wait_ge(M.tanh_ready, m + 1)
                if later(m):
                    v.wait_ge(M.glu_turned, m)
                v.scalar_tensor_tensor(tnh, tnh, 1.0, pm[2 + b][:, 0:DE], ALU.add, ALU.mult).then_inc(M.glu_step, 1)
                v.wait_ge(M.glu_step, m + 1)
                v.scalar_tensor_tensor(glu, tnh, 0.5, pm[2 + b][:, DE:2 * DE], ALU.mult, ALU.mult).then_inc(M.glu_ready, 1)

            def copy_out(m, b, u):
                v.wait_ge(M.glu_turned, m + 1)
                v.tensor_copy(gluT, pm[4][:, 0:DE].rearrange("p (k n) -> p k n", n=P)).then_inc(M.gluT_ready, 1)
                v.wait_ge(M.down_done, 2 * m + 1)
                if not isinstance(u, int) or u > 0:
                    v.wait_ge(y_stored[b], 16 * u)
                v.tensor_copy(yo[b][:, 0:512], pm[6][:, :]).then_inc(M.y0_ready, 1)

            def step_m(m, b, u):
                if not isinstance(m, int) or m < SLOT_TILES - 1:
                    copy_rows(m + 1, 1 - b, u + b)
                if later(m):
                    copy_out(m - 1, 1 - b, u - 1 + b)
                swiglu(m, b, u)

            copy_rows(0, 0, 0)
            run_slots(v, step_m, lambda: copy_out(SLOT_TILES - 1, 0, SLOT_TILES // 2))
            for t in range(NT):
                b, k = t % 2, 16 * (t // 2) + 16
                v.wait_ge(m_loaded[b], k)
                v.wait_ge(a_loaded[b], k)
                v.scalar_tensor_tensor(out_x[b], out_a[b], gate1[:, t:t + 1], out_x[b], ALU.mult, ALU.add).then_inc(M.half_summed, 1)
                v.wait_ge(M.half_summed, t + 1)
                v.wait_ge(b_loaded[b], k)
                v.scalar_tensor_tensor(out_x[b], out_b[b], gate2[:, t:t + 1], out_x[b], ALU.mult, ALU.add).then_inc(M.summed, 1)

        @block.gpsimd
        def _(g):
            made = ctx.enter_context(nc.semaphore("pool_made"))
            count = [0]

            def step(ins):
                count[0] += 1
                ins.then_inc(made, 1)
                g.wait_ge(made, count[0])

            def select(m, pattern, base, cm, op=ALU.is_ge, fill=0.0):
                step(g.affine_select(out=m, in_=m, pattern=pattern, compare_op=op, fill=fill, base=base,
                                     channel_multiplier=cm))

            step(g.memset(ones[:, :], 1.0))
            step(g.memset(ident[:, :], 0.0))
            select(ident[:, :], [[-1, P]], 0, 1, ALU.not_equal, 1.0)
            step(g.memset(upper[:, :], 1.0))
            select(upper[:, :], [[1, P]], 0, -1)
            step(g.memset(upper_strict[:, :], 1.0))
            select(upper_strict[:, :], [[1, P]], -1, -1)
            step(g.memset(level_mask[:, :, :], 1.0))
            for n, s_ in enumerate([1] + LEVELS):
                m = level_mask[:, n, :].rearrange("p (b r) -> p b r", r=2 * s_)
                nb = P // (2 * s_)
                select(m, [[-2 * s_, nb], [0, 2 * s_]], 0, 1)
                select(m, [[2 * s_, nb], [0, 2 * s_]], s_ - 1, -1)
                select(m, [[0, nb], [1, 2 * s_]], -s_, 0)
            step(g.memset(key_mask[:, :], 0.0))
            step(g.memset(key_mask[0:CH, CH:P], -BIG))
            step(g.memset(S[:, :, :], 0.0))
            step(g.memset(vWin[:, :, :, :], 0.0))
            step(g.memset(vWin[:, :, :, DH:DH + 1], 1.0))
            step(g.memset(kWin[:, :, :], 0.0))
            g.memset(ci[:, :, :], 0.0).then_inc(L.masks_made, 1)
            g.wait_ge(L.masks_made, 1)
            g.wait_ge(L.dve_consts, 1)

            def copy(dst, src):
                p, n = src.start_partition(), src.shape
                one = ones[p:p + n[0], 0:1] if len(n) == 2 else ones[p:p + n[0], 0:1].unsqueeze(2)
                return g.tensor_tensor(dst, src, one.broadcast_to(list(n)), ALU.mult)

            def halo(t):
                if later(t):
                    g.wait_ge(F.conv_done, t)
                copy(ci[:, :, 0:HALO], ci[:, :, P:P + HALO]).then_inc(F.halo_ready, 1)

            def front_tail(t):
                qk_in = tail[:, SQ0:SQ0 + QK].rearrange("p (h n) -> p h n", n=DH)
                g.wait_ge(F.chunk_copied, 6 * t + 6)
                if later(t):
                    g.wait_ge(F.qkn_ready, t)
                g.tensor_tensor(qkg[:, :, :], qk_in, qk_in, ALU.mult).then_inc(F.swa_squared, 1)
                g.wait_ge(F.swa_squared, t + 1)
                g.tensor_tensor(qk_in[:, 0:QH, :], qk_in[:, 0:QH, :],
                                gqk[:, None, 0:DH].broadcast_to([P, QH, DH]), ALU.mult)
                g.tensor_tensor(qk_in[:, QH:, :], qk_in[:, QH:, :],
                                gqk[:, None, DH:2 * DH].broadcast_to([P, KVH, DH]), ALU.mult).then_inc(F.swa_gained, 1)
                z = tail[:, Z0:Z0 + HP].rearrange("p (h n) -> p h n", h=H)
                g.wait_ge(F.tz_ready, t + 1)
                g.tensor_tensor(z, z, g_out[:, None, :].broadcast_to([P, H, P]), ALU.mult).then_inc(F.hz_ready, 1)
                g.wait_ge(F.qkvT_ready, t + 1)
                g.tensor_tensor(ctmp[:, 0:2 * H, :], qkvT[:, 0:2 * H, :], qkvT[:, 0:2 * H, :],
                                ALU.mult).then_inc(F.sq_ready, 1)

            def front(t):
                halo(t)
                front_tail(t)

            def both(t):
                back(t, t + 1)

            def back(t, nx=None):
                if later(t):
                    g.wait_ge(B.scores_done, t)
                copy(kWin[:, 1, :], kWin[:, 2, :]).then_inc(B.kOld_ready, 1)
                g.wait_ge(B.kOld_ready, t + 1)
                if later(t):
                    g.wait_ge(B.pv_done, t)
                copy(vWin[CH:P, 0, :, 0:DH], vWin[CH:P, 1, :, 0:DH]).then_inc(B.vOld_ready, 1)
                g.wait_ge(B.vOld_ready, t + 1)
                vin = tail[:, SV0:SV0 + KVH * DH].rearrange("p (h n) -> p h n", n=DH)
                copy(vWin[:, 1, :, 0:DH], vin)
                copy(vWin[0:CH, 0, :, 0:DH], vin[0:CH]).then_inc(B.vWin_ready, 1)
                g.wait_ge(B.kn_ready, t + 1)
                g.wait_ge(B.eg_ready, t + 1)
                g.wait_ge(B.kn_turned, t + 1)
                g.tensor_tensor(kd[:, :, :], kn[:, :, :], wide(bs[:, 4:8]), ALU.mult).then_inc(B.kd_ready, 1)
                g.wait_ge(B.aT_ready, t + 1)
                for l in range(len(LEVELS)):
                    if l > 1:
                        g.wait_ge(B.y_done, 6 * t + l - 1)
                    g.tensor_tensor(aTm[:, l % 2, :, :], aT[:, :, :],
                                    level_mask[:, l + 1:l + 2, :].broadcast_to([P, H, P]), ALU.mult).then_inc(B.aTm_ready, 1)
                if nx is not None:
                    halo(nx)
                g.wait_ge(B.o_ready, t + 1)
                g.tensor_tensor(o2[:, :, :], o[:, :, :], o[:, :, :], ALU.mult).then_inc(B.o_squared, 1)
                if nx is not None:
                    front_tail(nx)

            run_tiles(g, front, both, back)
            g.wait_ge(B.lg_ready, NT)
            step(g.iota(iota_i, [[1, P]], base=0, channel_multiplier=0))
            step(g.tensor_copy(iota_f, iota_i))
            step(g.iota(iota_i[:, 0:NT], [[P, NT]], base=0, channel_multiplier=0))
            step(g.tensor_copy(step_f, iota_i[:, 0:NT]))
            step(g.iota(iota_i[:, 0:NT], [[P, NT]], base=0, channel_multiplier=1))
            g.tensor_copy(tok_f, iota_i[:, 0:NT]).then_inc(R.iotas, 1)

            g.wait_ge(L.mid_stored, 32 * NT)
            g.wait_ge(R.idx_ready, 1)
            for m in range(SLOT_TILES):
                if m > 1:
                    g.wait_ge(M.turned, m - 1)
                g.indirect_dma_start(hg[m % 2], None, h_mid,
                                     bass.IndirectOffsetOnAxis(idx[:, m:m + 1], 0)).then_inc(gathered[m % 2], 16)
            for b in range(2):
                g.wait_ge(y_stored[b], 16 * ((SLOT_TILES + 1 - b) // 2))
            for t in range(NT):
                b = t % 2
                if t > 1:
                    g.wait_ge(M.summed, t - 1)
                g.indirect_dma_start(out_a[b], None, y_slots, bass.IndirectOffsetOnAxis(slots_i[:, t:t + 1], 0)).then_inc(a_loaded[b], 16)
                g.indirect_dma_start(out_b[b], None, y_slots, bass.IndirectOffsetOnAxis(slots_i[:, NT + t:NT + t + 1], 0)).then_inc(b_loaded[b], 16)


_INS = ["x", "attn_norm_g", "w_in", "conv_w", "gdn_a_log", "gdn_dt_bias", "gdn_out_norm_g", "swa_q_norm_g",
        "swa_k_norm_g", "swa_sinks", "w_out", "ffn_norm_g", "w_group", "b_group", "w_expert", "b_expert",
        "w_gate_up", "w_down"]


def kernel(**inputs):
    import concourse.bacc as bacc
    from concourse.bass_utils import run_bass_kernel_spmd

    nc = bacc.Bacc("TRN2", target_bir_lowering=False, num_devices=1)
    arrays, args = {}, []
    for name in _INS:
        a = np.ascontiguousarray(inputs[name])
        arrays[f"in_{name}"] = a
        args.append(nc.dram_tensor(f"in_{name}", a.shape, mybir.dt.from_np(a.dtype), kind="ExternalInput").ap())
    out = nc.dram_tensor("out", [1, T, D], F32, kind="ExternalOutput").ap()
    build(nc, *args, out)
    return run_bass_kernel_spmd(nc, [arrays], core_ids=[0]).results[0]["out"]
```

```python
from collections import namedtuple
from contextlib import ExitStack

import numpy as np

import concourse.bass as bass
from concourse import mybir

F32 = mybir.dt.float32
I32 = mybir.dt.int32
ALU = mybir.AluOpType
ACT = mybir.ActivationFunctionType
AX_X = mybir.AxisListType.X
P = 128
EPS = 1e-6

D = 1024
T = 1024
NT = T // P
KD = D // P
H = 4
HP = H * P
DPROJ = 2824
QH, KVH, DH = 8, 2, 64
GRP = QH // KVH
CH = 64
QK = (QH + KVH) * DH
Z0, AL0, BE0, SQ0 = 0, HP, HP + H, HP + 2 * H
SK0 = SQ0 + QH * DH
SV0 = SK0 + KVH * DH
TAIL = SV0 + KVH * DH
CHUNKS = [(0, 512), (512, 512), (1024, 512), (1536, 512), (2048, 512), (2560, 264)]
NC_ = len(CHUNKS)
BANK, TURN_BANK = [0, 1, 0, 0, 1, 0], [1, 0, 1]
KW = 4
HALO = KW - 1
GROUPS, EPG, NE, DE = 4, 4, 16, 256
NL = GROUPS + NE
TOPK = 2
SLOT_TILES = (TOPK * T - NE) // P + NE
LEVELS = [2, 4, 8, 16, 32, 64]
RSQRT_MAGIC = 0x5F3759DF
NSMALL = 16
VF, VB, VL = 29, 38, 12
BIG = 1e30


def build(nc, x, attn_norm_g, w_in, conv_w, a_log, dt_bias, out_norm_g, q_norm_g, k_norm_g, sinks,
          w_out, ffn_norm_g, w_group, b_group, w_expert, b_expert, w_gate_up, w_down, out, dbg=None):
    with ExitStack() as ctx:
        def sb(name, shape, dt=F32):
            return ctx.enter_context(nc.sbuf_tensor(name, [P] + shape, dt))

        def sems(names, about=""):
            return namedtuple("Signals", names)(*[ctx.enter_context(nc.semaphore(about + n)) for n in names.split()])

        x_mid = nc.dram_tensor("x_mid", [T, D], F32).ap()
        h_mid = nc.dram_tensor("h_mid", [T, D], F32).ap()
        y_slots = nc.dram_tensor("y_slots", [SLOT_TILES * P, D], F32).ap()

        w_sb = sb("w_sb", [KD, DPROJ])
        wo_sb = sb("wo_sb", [KD, D])
        ident = sb("ident", [P])
        ones = sb("ones", [P])
        upper = sb("upper", [P])
        upper_strict = sb("upper_strict", [P])
        level_mask = sb("level_mask", [1 + len(LEVELS), P])
        gain1 = sb("gain1", [KD])
        gain2 = sb("gain2", [KD])
        cw = sb("cw", [KW, 3 * H])
        rows = sb("rows", [2 * DH + P + 3 * H + QH + NL])
        GQ, GO, DT, AL, SI, BL = np.cumsum([0, 2 * DH, P, H, H, QH]).tolist()
        gqk = rows[:, GQ:GQ + 2 * DH]
        g_out = rows[:, GO:GO + P]
        dtb = rows[:, DT:DT + H]
        neg_a = rows[:, AL:AL + H]
        sink = rows[:, SI:SI + QH]
        b_rt = rows[:, BL:BL + NL]
        w_rt = sb("w_rt", [KD, NL])
        key_mask = sb("key_mask", [P])

        xt = sb("xt", [D])
        hT = sb("hT", [KD, P])
        pqkv = sb("pqkv", [3 * HP])
        tail = sb("tail", [TAIL])
        ci = sb("ci", [3 * H, HALO + P])
        cv = pqkv[:, :].rearrange("p (h n) -> p h n", n=P)
        qkvT = sb("qkvT", [3 * H, P])
        qkn = sb("qkn", [QH + KVH, DH])
        gsz = sb("gsz", [H, P])
        fs = sb("fs", [80])
        kn = sb("kn", [H, P])
        vt = sb("vt", [H, P])
        knT = sb("knT", [H, P])
        ctmp = sb("ctmp", [3 * H, P])
        dT, aT = ctmp[:, 0:H, :], ctmp[:, H:2 * H, :]
        XT = sb("XT", [H, P])
        qkT = sb("qkT", [H, P])
        aTm = sb("aTm", [2, H, P])
        qkg = aTm[:, :, :, :].rearrange("p a h n -> p (a h n)")[:, 0:QK].rearrange("p (h n) -> p h n", n=DH)
        X = sb("X", [H, P])
        Y = sb("Y", [H, P])
        V = sb("V", [H, P])
        S = sb("S", [H, P])
        bs = sb("bs", [112])
        qT = V
        kWin = sb("kWin", [3, CH])
        vWin = sb("vWin", [2, KVH, DH + 1])
        lg = sb("lg", [NT, NL])
        free = w_sb[:, :, :].rearrange("p k n -> p (k n)")
        taken = [0]

        def part(*shape):
            n = int(np.prod(shape))
            a = free[:, taken[0]:taken[0] + n]
            taken[0] += n
            assert taken[0] <= KD * DPROJ
            if len(shape) == 2:
                return a.rearrange("p (a b) -> p a b", a=shape[0])
            if len(shape) == 3:
                return a.rearrange("p (a b c) -> p a b c", a=shape[0], b=shape[1])
            return a

        wgu = [part(KD, 2 * DE) for _ in range(2)]
        wdn = [part(DE // P, D) for _ in range(2)]
        hg = [part(D) for _ in range(2)]
        hgT = [part(KD, P) for _ in range(2)]
        yo = [part(D) for _ in range(2)]
        tnh, glu, gluT = part(DE), part(DE), part(DE // P, P)
        gmax, m1, m2, sump, gate1, gate2, seen = [part(NT) for _ in range(7)]
        og, es, e1, e2 = [part(NT, GROUPS) for _ in range(4)]
        ex = part(NT * GROUPS + NT)
        prod, pick1, pick2, both_picks = [part(NT, GROUPS, EPG) for _ in range(4)]
        run, slot = part(NT + 1, NE), part(NT, NE)
        over = part(NE, NT)
        tiles_of, tiles_to, base = part(NE), part(NE), part(NE)
        slots = part(TOPK * NT)
        slots_i, mod_i, div_i = [part(TOPK * NT).bitcast(I32) for _ in range(3)]
        mod_f, div_f = part(TOPK * NT), part(TOPK * NT)
        iota_i = part(P).bitcast(I32)
        iota_f, tok_f = part(P), part(NT)
        step_f = part(NT)
        past = part(SLOT_TILES + 1, NE)
        texp_f, texp = part(SLOT_TILES + 1), part(SLOT_TILES + 1).bitcast(I32)
        idx = part(SLOT_TILES + 1).bitcast(I32)
        hot_mod = [hgT[u // 8].rearrange("p k n -> p (k n)")[:, (u % 8) * P:(u % 8 + 1) * P] for u in range(TOPK * NT)]
        hot_div = yo[0][:, 0:TOPK * NT * 32].rearrange("p (u m) -> p u m", m=32)
        out_a = [wgu[b][:, 0:2, :].rearrange("p k n -> p (k n)") for b in range(2)]
        out_b = [wgu[b][:, 2:4, :].rearrange("p k n -> p (k n)") for b in range(2)]
        out_x = [wgu[b][:, 4:6, :].rearrange("p k n -> p (k n)") for b in range(2)]
        y_mix = sb("y_mix", [D])
        sc = sb("sc", [QH, P])
        pT = sb("pT", [QH, P])
        xr = sc[:, :, :].rearrange("p h n -> p (h n)")
        yT, hT2, r, o, o2, kd = pT, pT, vt, X, Y, kn

        pm = [ctx.enter_context(nc.psum_tensor(f"pm{i}", [P, 512], F32)) for i in range(8)]

        def heads(bank, n=P):
            return bank[:, 0:4 * n].rearrange("p (h n) -> p h n", h=4)

        def wide(ap4, n=P):
            return ap4.unsqueeze(2).broadcast_to([P, ap4.shape[1], n])

        L = sems("consts_loaded masks_made weights_ready state_zeroed dve_consts x_loaded xr_loaded mid_stored masked")
        w_loaded = [ctx.enter_context(nc.semaphore(f"w_loaded{c}")) for c in range(NC_)]
        wo_loaded = ctx.enter_context(nc.semaphore("wo_loaded"))
        F = sems("ssx_ready h_scaled h_turned hT_ready chunk_done chunk_copied turned ci_copied halo_ready conv_step"
                 " conv_done tanh_ready qkvT_ready sq_ready swa_squared swa_gained qkn_ready u_ready"
                 " exp_ready ln_ready la_ready tz_ready hz_ready gsz_ready front_step")
        B = sems("kv_turned small_done gi_done kn_ready vt_ready kn_turned knT_ready diff_ready dT_exp dT_ready"
                 " eg_ready kk_done qk_done aT_ready qkT_ready aTm_ready xT0_ready x0_turned x0_copied y_done"
                 " y_copied z_done zt_done x_updated xT_updated ks_done r_ready v0_done v_ready o2_done kd_ready s_done s_updated"
                 " o_ready o_squared ya_ready swa_turned qT_ready kWin_ready kOld_ready vOld_ready vWin_ready scores_done"
                 " top_found sc_ready p_ready p_turned pT_ready pv_done sink_in sink_exp yb_ready y_turned yT_ready out_done"
                 " xm_ready ss2_ready hm_ready hm_turned hT2_ready logits_done lg_ready back_step late_step")

        R = sems("iotas route_step exp_in exp_out picks counts hots idx_summed idx_ready ready", "route_")
        M = sems("turned hT_ready gu_done tanh_ready glu_step glu_ready glu_turned gluT_ready down_done"
                 " y0_ready y1_ready half_summed summed", "slots_")
        gathered, w1_loaded, w2_loaded, y_stored, a_loaded, b_loaded, m_loaded, out_stored = [
            [ctx.enter_context(nc.semaphore(f"{n}{b}")) for b in range(2)]
            for n in "gathered w1_loaded w2_loaded y_stored a_loaded b_loaded m_loaded out_stored".split()]

        def run_slots(eng, step, last):
            step(0, 0, 0)
            with eng.Fori(0, SLOT_TILES // 2 - 1) as u:
                step(2 * u + 1, 1, u)
                step(2 * u + 2, 0, u + 1)
            step(SLOT_TILES - 2, 1, SLOT_TILES // 2 - 1)
            step(SLOT_TILES - 1, 0, SLOT_TILES // 2)
            last()

        block = ctx.enter_context(nc.Block())

        def later(t):
            return not isinstance(t, int) or t > 0

        def run_tiles(front, body, late, eng):
            front(0)
            body(0, 1, None)
            with eng.Fori(1, NT - 1) as i:
                body(i, i + 1, i - 1)
            body(NT - 1, None, NT - 2)
            late(NT - 1)

        @block.sync
        def _(sp):
            def col(ap1, n):
                return ap1.rearrange("(k p) -> p k", p=P)

            small = [
                (gain1[:, :], attn_norm_g[0].rearrange("(k p) -> p k", p=P)),
                (gain2[:, :], ffn_norm_g[0].rearrange("(k p) -> p k", p=P)),
            ]
            small += [(cw[:, j, :], conv_w[0, j].rearrange("(k p) -> p k", p=P)) for j in range(KW)]
            small += [
                (gqk[:, 0:DH], q_norm_g.broadcast_to([P, DH])),
                (gqk[:, DH:2 * DH], k_norm_g.broadcast_to([P, DH])),
                (g_out, out_norm_g.broadcast_to([P, P])),
                (dtb, dt_bias.broadcast_to([P, H])),
                (neg_a, a_log.broadcast_to([P, H])),
                (sink, sinks.broadcast_to([P, QH])),
                (b_rt[:, 0:GROUPS], b_group.broadcast_to([P, GROUPS])),
                (b_rt[:, GROUPS:NL], b_expert.broadcast_to([P, NE])),
                (w_rt[:, :, 0:GROUPS], w_group[0].rearrange("(k p) n -> p k n", p=P)),
                (w_rt[:, :, GROUPS:NL], w_expert[0].rearrange("(k p) n -> p k n", p=P)),
            ]
            sp.dma_start(xt[:, :], x[0, 0:P, :]).then_inc(L.x_loaded, 16)
            for dst, src in small:
                sp.dma_start(dst, src, allow_slow_non_contiguous=True).then_inc(L.consts_loaded, 16)
            for c, (c0, n) in enumerate(CHUNKS):
                sp.dma_start(w_sb[:, :, c0:c0 + n],
                             w_in[0, :, c0:c0 + n].rearrange("(k p) n -> p k n", p=P)).then_inc(w_loaded[c], 16)
            sp.dma_start(wo_sb[:, :, :], w_out[0].rearrange("(k p) n -> p k n", p=P)).then_inc(wo_loaded, 16)

            def store(t):
                sp.wait_ge(B.xm_ready, 2 * t + 2)
                sp.dma_start(x_mid[bass.ts(t, P), :], xr).then_inc(L.mid_stored, 16)
                sp.wait_ge(B.hm_ready, t + 1)
                sp.dma_start(h_mid[bass.ts(t, P), :], y_mix[:, :]).then_inc(L.mid_stored, 16)

            def body(t, nx, pv):
                if nx is not None:
                    sp.wait_ge(F.h_turned, t + 1)
                    sp.dma_start(xt[:, :], x[0, bass.ts(nx, P), :]).then_inc(L.x_loaded, 16)
                if pv is not None:
                    store(pv)
                sp.wait_ge(B.p_turned, t + 1)
                sp.dma_start(xr, x[0, bass.ts(t, P), :]).then_inc(L.xr_loaded, 16)

            run_tiles(lambda t: None, body, store, sp)
            sp.wait_ge(L.mid_stored, 32 * NT)

            def load_w1(m, b):
                e = sp.value_load(texp[0:1, bass.ds(m, 1)], min_val=0, max_val=NE - 1)
                if not isinstance(m, int) or m > 1:
                    sp.wait_ge(M.gu_done, m - 1)
                sp.dma_start(wgu[b], w_gate_up[0, bass.ds(e, 1)].rearrange("o (k p) n -> p (o k) n", p=P)).then_inc(w1_loaded[b], 16)

            def load_w2(m, b):
                e = sp.value_load(texp[0:1, bass.ds(m, 1)], min_val=0, max_val=NE - 1)
                if not isinstance(m, int) or m > 1:
                    sp.wait_ge(M.down_done, 2 * m - 2)
                sp.dma_start(wdn[b], w_down[0, bass.ds(e, 1)].rearrange("o (k p) n -> p (o k) n", p=P)).then_inc(w2_loaded[b], 16)

            def store_y(m, b):
                sp.wait_ge(M.y0_ready, m + 1)
                sp.wait_ge(M.y1_ready, m + 1)
                sp.dma_start(y_slots[bass.ts(m, P), :], yo[b]).then_inc(y_stored[b], 16)

            sp.wait_ge(R.ready, 1)
            load_w1(0, 0)
            load_w2(0, 0)
            load_w1(1, 1)
            load_w2(1, 1)
            load_w1(2, 0)
            with sp.Fori(0, SLOT_TILES // 2 - 1) as u:
                load_w1(2 * u + 3, 1)
                load_w2(2 * u + 2, 0)
                store_y(2 * u, 0)
                load_w1(2 * u + 4, 0)
                load_w2(2 * u + 3, 1)
                store_y(2 * u + 1, 1)
            load_w2(SLOT_TILES - 1, 0)
            for m in range(SLOT_TILES - 3, SLOT_TILES):
                store_y(m, m % 2)
            for b in range(2):
                sp.wait_ge(y_stored[b], 16 * ((SLOT_TILES + 1 - b) // 2))
            for t in range(NT):
                if t > 1:
                    sp.wait_ge(out_stored[t % 2], 16 * (t // 2))
                sp.dma_start(out_x[t % 2], x_mid[t * P:(t + 1) * P, :]).then_inc(m_loaded[t % 2], 16)
                if t:
                    sp.wait_ge(M.summed, t)
                    sp.dma_start(out[0, (t - 1) * P:t * P, :], out_x[(t - 1) % 2]).then_inc(out_stored[(t - 1) % 2], 16)
            sp.wait_ge(M.summed, NT)
            sp.dma_start(out[0, (NT - 1) * P:, :], out_x[1]).then_inc(out_stored[1], 16)
            for b in range(2):
                sp.wait_ge(out_stored[b], 16 * NT // 2)

        @block.tensor
        def _(pe):
            def mm(o_, l_, r_, start=True, stop=True):
                return pe.matmul(o_, lhsT=l_, rhs=r_, start=start, stop=stop, skip_group_check=True)

            def turn(o_, in_):
                return pe.transpose(o_, in_, ident[:, :])

            def turn_h(t):
                pe.wait_ge(F.h_scaled, t + 1)
                if not isinstance(t, int) or t:
                    pe.wait_ge(F.chunk_copied, 6 * t)
                for k in range(KD):
                    ins = turn(pm[k // 4][:, (k % 4) * P:(k % 4 + 1) * P], xt[:, k * P:(k + 1) * P])
                ins.then_inc(F.h_turned, 1)

            def project(t, c):
                c0, n = CHUNKS[c]
                if c < 2:
                    pe.wait_ge(F.hT_ready, 2 * t + 2)
                elif c == 2:
                    pe.wait_ge(F.chunk_copied, 6 * t + 1)
                elif c < 5:
                    pe.wait_ge(F.ci_copied, 3 * t + c - 1)
                else:
                    pe.wait_ge(F.chunk_copied, 6 * t + 4)
                if isinstance(t, int) and t == 0:
                    pe.wait_ge(w_loaded[c], 16)
                for k in range(KD):
                    ins = mm(pm[BANK[c]][:, 0:n], hT[:, k, :], w_sb[:, k, c0:c0 + n], k == 0, k == KD - 1)
                ins.then_inc(F.chunk_done, 1)

            def turn_qkv(t, j):
                if j < 2:
                    pe.wait_ge(F.chunk_copied, 6 * t + j + 2)
                else:
                    pe.wait_ge(F.chunk_copied, 6 * t + 3)
                    pe.wait_ge(F.ci_copied, 3 * t + 1)
                for h in range(H):
                    ins = turn(pm[TURN_BANK[j]][:, h * P:(h + 1) * P], pqkv[:, (H * j + h) * P:(H * j + h + 1) * P])
                ins.then_inc(F.turned, 1)

            def front(t):
                turn_h(t)
                for c in range(3):
                    project(t, c)
                for j in range(3):
                    turn_qkv(t, j)
                for c in range(3, NC_):
                    project(t, c)

            def turn_y(t):
                pe.wait_ge(B.ya_ready, t + 1)
                pe.wait_ge(B.yb_ready, t + 1)
                for k in range(KD):
                    ins = turn(pm[6 + k // 4][:, (k % 4) * P:(k % 4 + 1) * P], y_mix[:, k * P:(k + 1) * P])
                ins.then_inc(B.y_turned, 1)

            def out_half(t, n):
                pe.wait_ge(B.yT_ready, t + 1)
                if isinstance(t, int) and t == 0:
                    pe.wait_ge(wo_loaded, 16)
                for k in range(KD):
                    ins = mm(pm[6 + n][:, :], yT[:, k, :], wo_sb[:, k, n * 512:(n + 1) * 512], k == 0, k == KD - 1)
                ins.then_inc(B.out_done, 1)

            def turn_hm(t):
                pe.wait_ge(B.hm_ready, t + 1)
                for k in range(KD):
                    ins = turn(pm[6 + k // 4][:, (k % 4) * P:(k % 4 + 1) * P], y_mix[:, k * P:(k + 1) * P])
                ins.then_inc(B.hm_turned, 1)

            def logits(t):
                pe.wait_ge(B.hT2_ready, 2 * t + 2)
                for k in range(KD):
                    ins = mm(pm[6][:, 0:NL], hT2[:, k, :], w_rt[:, k, :], k == 0, k == KD - 1)
                ins.then_inc(B.logits_done, 1)

            def late(t):
                turn_y(t)
                out_half(t, 0)
                out_half(t, 1)
                turn_hm(t)
                logits(t)

            def body(t, nx, pv):
                def ahead(c):
                    if nx is not None:
                        project(nx, c)

                if nx is not None:
                    turn_h(nx)
                if pv is not None:
                    turn_y(pv)
                ahead(0)
                pe.wait_ge(F.qkvT_ready, t + 1)
                if later(t):
                    pe.wait_ge(B.xT_updated, 6 * t)
                    pe.wait_ge(B.v_ready, t)
                    pe.wait_ge(B.o_ready, t)
                    pe.wait_ge(B.s_updated, t)
                for h in range(H):
                    turn(pm[2][:, h * P:(h + 1) * P], qkvT[:, H + h, :])
                for h in range(H):
                    ins = turn(pm[3][:, h * P:(h + 1) * P], qkvT[:, 2 * H + h, :])
                ins.then_inc(B.kv_turned, 1)
                pe.wait_ge(F.la_ready, t + 1)
                la = fs[:, 20:20 + H]
                for h in range(H):
                    ins = mm(pm[5][:, h * P:(h + 1) * P], la[:, h:h + 1].broadcast_to([P, P]), upper[:, :])
                ins.then_inc(B.gi_done, 1)
                mm(pm[4][:, 8:8 + H], upper[:, :], la)
                mm(pm[4][:, 12:12 + H], ones[:, :], la)
                pe.wait_ge(F.sq_ready, t + 1)
                for h in range(2 * H):
                    ins = mm(pm[4][:, h:h + 1], ctmp[:, h, :], ones[:, 0:1])
                ins.then_inc(B.small_done, 1)
                if pv is not None:
                    out_half(pv, 0)
                else:
                    ahead(1)
                pe.wait_ge(B.kn_ready, t + 1)
                for h in range(H):
                    ins = turn(pm[2][:, h * P:(h + 1) * P], kn[:, h, :])
                ins.then_inc(B.kn_turned, 1)
                if pv is not None:
                    out_half(pv, 1)
                pe.wait_ge(B.knT_ready, t + 1)
                pe.wait_ge(B.vt_ready, t + 1)
                for h in range(H):
                    ins = mm(pm[3][:, h * P:(h + 1) * P], knT[:, h, :], knT[:, h, :])
                ins.then_inc(B.kk_done, 1)
                pe.wait_ge(B.diff_ready, t + 1)
                for h in range(H):
                    ins = mm(pm[5][:, h * P:(h + 1) * P], knT[:, h, :], qkvT[:, h, :])
                ins.then_inc(B.qk_done, 1)
                if pv is not None:
                    ahead(1)
                pe.wait_ge(B.xT0_ready, t + 1)
                for h in range(H):
                    ins = turn(pm[2][:, h * P:(h + 1) * P], XT[:, h, :])
                ins.then_inc(B.x0_turned, 1)
                if pv is not None:
                    turn_hm(pv)
                pe.wait_ge(B.x0_copied, t + 1)
                n = len(LEVELS)
                for l in range(n):
                    pe.wait_ge(B.aTm_ready, 6 * t + l + 1)
                    if l:
                        pe.wait_ge(B.x_updated, 5 * t + l)
                    else:
                        pe.wait_ge(B.aT_ready, t + 1)
                    for h in range(H):
                        ins = mm(pm[3][:, h * P:(h + 1) * P], aTm[:, l % 2, h, :], X[:, h, :])
                    ins.then_inc(B.y_done, 1)
                    if l == 0:
                        if later(t):
                            pe.wait_ge(B.s_updated, t)
                        for h in range(H):
                            ins = mm(pm[4][:, h * P:(h + 1) * P], knT[:, h, :], S[:, h, :])
                        ins.then_inc(B.ks_done, 1)
                        if pv is not None:
                            logits(pv)
                    elif l == 1:
                        ahead(2)
                    elif l == 2:
                        pe.wait_ge(F.qkn_ready, t + 1)
                        if later(t):
                            pe.wait_ge(B.lg_ready, t)
                        for g in range(GRP):
                            turn(pm[6][:, g * P:(g + 1) * P],
                                 qkn[:, KVH * g:KVH * g + KVH, :].rearrange("p h d -> p (h d)"))
                        turn(pm[7][:, 0:P], qkn[:, QH:QH + KVH, :].rearrange("p h d -> p (h d)")).then_inc(B.swa_turned, 1)
                        if nx is not None:
                            for j in range(3):
                                turn_qkv(nx, j)
                    elif l == 3:
                        ahead(3)
                    elif l == 4:
                        ahead(4)
                    elif l == 5:
                        pe.wait_ge(B.p_ready, t + 1)
                        for h in range(QH):
                            ins = turn(pm[6 + h // 4][:, (h % 4) * P:(h % 4 + 1) * P], sc[:, h, :])
                        ins.then_inc(B.p_turned, 1)
                    pe.wait_ge(B.y_copied, 6 * t + l + 1)
                    if l:
                        pe.wait_ge(B.xT_updated, 6 * t + l)
                    if l < n - 1:
                        for h in range(H):
                            ins = mm(pm[2][:, h * P:(h + 1) * P], XT[:, h, :], Y[:, h, :])
                    else:
                        for h in range(H):
                            ins = mm(pm[2][:, h * P:(h + 1) * P], qkvT[:, h, :], S[:, h, :])
                    ins.then_inc(B.z_done, 1)
                    if l == 0:
                        pe.wait_ge(B.qkT_ready, t + 1)
                    for h in range(H):
                        ins = mm(pm[5][:, h * P:(h + 1) * P], Y[:, h, :], XT[:, h, :])
                    ins.then_inc(B.zt_done, 1)
                    if l == 2:
                        pe.wait_ge(B.qT_ready, t + 1)
                        pe.wait_ge(B.kWin_ready, t + 1)
                        mm(pm[6][:, 0:P], ident[:, :], ident[:, :])
                        for kv in range(KVH):
                            for half in range(2):
                                keys = kWin[kv * DH:(kv + 1) * DH, 0:3:1 + half, :]
                                if half == 0:
                                    keys = kWin[kv * DH:(kv + 1) * DH, 0:2, :]
                                for g in range(GRP):
                                    ins = mm(pm[6 + kv][half * CH:(half + 1) * CH, g * P:(g + 1) * P],
                                             qT[kv * DH:(kv + 1) * DH, g, half * CH:(half + 1) * CH], keys)
                        ins.then_inc(B.scores_done, 1)
                pe.wait_ge(B.pT_ready, t + 1)
                pe.wait_ge(B.vWin_ready, t + 1)
                for half in range(2):
                    for h in range(QH):
                        kv, g = h // GRP, h % GRP
                        ins = mm(pm[6 + kv][half * CH:(half + 1) * CH, g * (DH + 1):(g + 1) * (DH + 1)],
                                 pT[:, h, half * CH:(half + 1) * CH], vWin[:, half, kv, :])
                ins.then_inc(B.pv_done, 1)
                pe.wait_ge(B.xT_updated, 6 * t + 6)
                pe.wait_ge(B.r_ready, t + 1)
                for h in range(H):
                    ins = mm(pm[3][:, h * P:(h + 1) * P], XT[:, h, :], r[:, h, :])
                ins.then_inc(B.v0_done, 1)
                ahead(5)
                pe.wait_ge(B.v_ready, t + 1)
                pe.wait_ge(B.kd_ready, t + 1)
                for h in range(H):
                    ins = mm(pm[5][:, h * P:(h + 1) * P], kd[:, h, :], V[:, h, :])
                ins.then_inc(B.s_done, 1)
                for h in range(H):
                    ins = mm(pm[4][:, h * P:(h + 1) * P], qkT[:, h, :], V[:, h, :])
                ins.then_inc(B.o2_done, 1)

            pe.wait_ge(L.masks_made, 1)
            pe.wait_ge(L.consts_loaded, 16 * NSMALL)
            run_tiles(front, body, late, pe)

            pe.wait_ge(R.picks, 1)
            picks = both_picks.rearrange("p t g e -> p (t g e)")
            mm(pm[0][:, 0:P], upper_strict[:, :], picks)
            mm(pm[0][:, P:2 * P], ones[:, :], picks).then_inc(R.counts, 1)
            pe.wait_ge(R.hots, 1)
            for u in range(TOPK * NT):
                ins = mm(pm[1][:, 0:32], hot_mod[u], hot_div[:, u, :], u == 0, u == TOPK * NT - 1)
            ins.then_inc(R.idx_summed, 1)

            def turn_rows(m, b, u):
                pe.wait_ge(gathered[b], 16 * u + 16)
                if later(m):
                    pe.wait_ge(M.hT_ready, 2 * m)
                for k in range(KD):
                    ins = turn(pm[k // 4][:, (k % 4) * P:(k % 4 + 1) * P], hg[b][:, k * P:(k + 1) * P])
                ins.then_inc(M.turned, 1)

            def gate_up(m, b, u):
                pe.wait_ge(M.hT_ready, 2 * m + 2)
                pe.wait_ge(w1_loaded[b], 16 * u + 16)
                for k in range(KD):
                    ins = mm(pm[2 + b][:, :], hgT[b][:, k, :], wgu[b][:, k, :], k == 0, k == KD - 1)
                ins.then_inc(M.gu_done, 1)

            def down(m, b, u):
                pe.wait_ge(M.glu_ready, m + 1)
                for k in range(DE // P):
                    ins = turn(pm[4][:, k * P:(k + 1) * P], glu[:, k * P:(k + 1) * P])
                ins.then_inc(M.glu_turned, 1)
                pe.wait_ge(w2_loaded[b], 16 * u + 16)
                if later(m):
                    pe.wait_ge(M.y0_ready, m)
                    pe.wait_ge(M.y1_ready, m)
                pe.wait_ge(M.gluT_ready, m + 1)
                for n in range(2):
                    for k in range(DE // P):
                        ins = mm(pm[6 + n][:, :], gluT[:, k, :], wdn[b][:, k, n * 512:(n + 1) * 512], k == 0,
                                 k == DE // P - 1)
                    ins.then_inc(M.down_done, 1)

            def step(m, b, u):
                if not isinstance(m, int) or m < SLOT_TILES - 1:
                    turn_rows(m + 1, 1 - b, u + b)
                gate_up(m, b, u)
                if later(m):
                    down(m - 1, 1 - b, u - 1 + b)

            turn_rows(0, 0, 0)
            run_slots(pe, step, lambda: down(SLOT_TILES - 1, 0, SLOT_TILES // 2))

        @block.scalar
        def _(act):
            def square_x(t):
                act.wait_ge(L.x_loaded, 16 * t + 16)
                act.activation(hT[:, :, :], xt[:, :].rearrange("p (k n) -> p k n", n=P), ACT.Square, accum_out=fs[:, 0:1]).then_inc(F.ssx_ready, 1)

            def copy_chunk(t, c):
                c0, n = CHUNKS[c]
                act.wait_ge(F.chunk_done, 6 * t + c + 1)
                dst = pqkv[:, c0:c0 + n] if c < 3 else tail[:, c0 - 3 * HP:c0 - 3 * HP + n]
                if c == 3 and later(t):
                    act.wait_ge(F.gsz_ready, t)
                    act.wait_ge(F.qkn_ready, t)
                    act.wait_ge(F.la_ready, t)
                    act.wait_ge(B.vWin_ready, t)
                act.activation(dst, pm[BANK[c]][:, 0:n], ACT.Copy).then_inc(F.chunk_copied, 1)

            def copy_ci(t, j):
                act.wait_ge(F.turned, 3 * t + j + 1)
                if j == 0:
                    act.wait_ge(F.halo_ready, t + 1)
                act.activation(ci[:, H * j:H * j + H, HALO:HALO + P], heads(pm[TURN_BANK[j]]), ACT.Copy).then_inc(F.ci_copied, 1)

            def gates(t):
                act.wait_ge(F.u_ready, t + 1)
                act.activation(fs[:, 12:12 + H], fs[:, 8:8 + H], ACT.Exp).then_inc(F.exp_ready, 1)
                act.wait_ge(F.exp_ready, t + 1)
                act.activation(fs[:, 16:16 + H], fs[:, 12:12 + H], ACT.Ln, bias=1.0).then_inc(F.ln_ready, 1)
                act.activation(fs[:, 24:24 + H], tail[:, BE0:BE0 + H], ACT.Tanh, scale=0.5)
                if later(t):
                    act.wait_ge(B.ya_ready, t)
                act.activation(gsz[:, :, :], tail[:, Z0:Z0 + HP].rearrange("p (h n) -> p h n", h=H), ACT.Tanh,
                               scale=0.5).then_inc(F.tz_ready, 1)

            def swa_squares(t):
                act.wait_ge(F.chunk_copied, 6 * t + 6)
                if later(t):
                    act.wait_ge(B.xT_updated, 6 * t)
                act.activation(qkg, tail[:, SQ0:SQ0 + QK].rearrange("p (h n) -> p h n", n=DH),
                               ACT.Square).then_inc(F.swa_squared, 1)

            def silu(t):
                act.wait_ge(F.conv_done, t + 1)
                act.activation(ctmp[:, :, :], cv[:, :, :], ACT.Tanh).then_inc(F.tanh_ready, 1)

            def squares(t):
                act.wait_ge(F.qkvT_ready, t + 1)
                act.activation(ctmp[:, 0:2 * H, :], qkvT[:, 0:2 * H, :], ACT.Square).then_inc(F.sq_ready, 1)

            def front(t):
                square_x(t)
                for c in range(3):
                    copy_chunk(t, c)
                for j in range(3):
                    copy_ci(t, j)
                for c in range(3, NC_):
                    copy_chunk(t, c)
                swa_squares(t)
                gates(t)
                silu(t)
                squares(t)

            def copy_yT(t):
                act.wait_ge(B.y_turned, t + 1)
                act.activation(yT[:, 0:4, :], heads(pm[6]), ACT.Copy)
                act.activation(yT[:, 4:8, :], heads(pm[7]), ACT.Copy).then_inc(B.yT_ready, 1)

            def square_xm(t):
                act.wait_ge(B.xm_ready, 2 * t + 2)
                act.activation(y_mix[:, :], xr, ACT.Square, accum_out=bs[:, 88:89]).then_inc(B.ss2_ready, 1)

            def late(t):
                copy_yT(t)
                square_xm(t)

            def body(t, nx, pv):
                def ahead(c):
                    if nx is not None:
                        copy_chunk(nx, c)

                if nx is not None:
                    square_x(nx)
                if pv is not None:
                    copy_yT(pv)
                ahead(0)
                act.wait_ge(B.kv_turned, t + 1)
                act.activation(vt[:, :, :], heads(pm[3]), ACT.Copy).then_inc(B.vt_ready, 1)
                act.wait_ge(B.diff_ready, t + 1)
                act.activation(dT[:, :, :], dT[:, :, :], ACT.Exp).then_inc(B.dT_exp, 1)
                act.activation(bs[:, 0:3 * H], bs[:, 12:12 + 3 * H], ACT.Exp).then_inc(B.eg_ready, 1)
                if pv is None:
                    ahead(1)
                act.wait_ge(B.kn_turned, t + 1)
                act.activation(knT[:, :, :], heads(pm[2]), ACT.Copy).then_inc(B.knT_ready, 1)
                if pv is not None:
                    square_xm(pv)
                    ahead(1)
                act.wait_ge(B.x0_turned, t + 1)
                act.activation(X[:, :, :], heads(pm[2]), ACT.Copy).then_inc(B.x0_copied, 1)
                for l in range(len(LEVELS)):
                    act.wait_ge(B.y_done, 6 * t + l + 1)
                    act.activation(Y[:, :, :], heads(pm[3]), ACT.Copy).then_inc(B.y_copied, 1)
                    if l == 1:
                        ahead(2)
                    if l == 2:
                        act.wait_ge(B.swa_turned, t + 1)
                        act.activation(qT[:, :, :], heads(pm[6]), ACT.Copy).then_inc(B.qT_ready, 1)
                        act.wait_ge(B.kOld_ready, t + 1)
                        act.activation(kWin[:, 0:3:2, :], pm[7][:, 0:P].rearrange("p (a b) -> p a b", a=2),
                                       ACT.Copy).then_inc(B.kWin_ready, 1)
                        if nx is not None:
                            for j in range(3):
                                copy_ci(nx, j)
                    if l == 3:
                        ahead(3)
                    if l == 4:
                        act.wait_ge(B.sc_ready, t + 1)
                        act.activation(sc[:, :, :], sc[:, :, :], ACT.Exp, scale=DH ** -0.5).then_inc(B.p_ready, 1)
                        act.activation(bs[:, 56:64], bs[:, 48:56], ACT.Exp, scale=DH ** -0.5).then_inc(B.sink_exp, 1)
                        ahead(4)
                act.wait_ge(B.p_turned, t + 1)
                act.activation(pT[:, 0:4, :], heads(pm[6]), ACT.Copy)
                act.activation(pT[:, 4:8, :], heads(pm[7]), ACT.Copy).then_inc(B.pT_ready, 1)
                ahead(5)
                if nx is not None:
                    swa_squares(nx)
                    silu(nx)
                    gates(nx)
                    squares(nx)

            act.wait_ge(L.consts_loaded, 16 * NSMALL)
            act.activation(neg_a, neg_a, ACT.Exp).then_inc(L.weights_ready, 1)
            run_tiles(front, body, late, act)
            act.wait_ge(R.exp_in, 1)
            act.activation(ex, ex, ACT.Exp).then_inc(R.exp_out, 1)

            def step(m, b, u):
                act.wait_ge(M.gu_done, m + 1)
                if later(m):
                    act.wait_ge(M.glu_ready, m)
                act.activation(tnh, pm[2 + b][:, 0:DE], ACT.Tanh, scale=0.5).then_inc(M.tanh_ready, 1)
                if later(m):
                    copy_out(m - 1, 1 - b, u - 1 + b)

            def copy_out(m, b, u):
                act.wait_ge(M.down_done, 2 * m + 2)
                if not isinstance(u, int) or u > 0:
                    act.wait_ge(y_stored[b], 16 * u)
                act.activation(yo[b][:, 512:], pm[7][:, :], ACT.Copy).then_inc(M.y1_ready, 1)

            run_slots(act, step, lambda: copy_out(SLOT_TILES - 1, 0, SLOT_TILES // 2))

        @block.vector
        def _(v):
            def stepper(sem, t, per):
                count = [0]

                def step(ins):
                    count[0] += 1
                    ins.then_inc(sem, 1)
                    v.wait_ge(sem, per * t + count[0])
                return step, count

            def rsqrt(step, y, a, tmp, src, scale):
                step(v.tensor_scalar(a, src, scale, EPS, ALU.mult, ALU.add))
                step(v.tensor_scalar(y.bitcast(I32), a.bitcast(I32), 1, None, ALU.logical_shift_right))
                step(v.tensor_scalar(y.bitcast(I32), y.bitcast(I32), -1, RSQRT_MAGIC, ALU.mult, ALU.add))
                for _i in range(3):
                    step(v.tensor_tensor(tmp, y, y, ALU.mult))
                    step(v.scalar_tensor_tensor(tmp, tmp, -0.5, a, ALU.mult, ALU.mult))
                    step(v.scalar_tensor_tensor(y, tmp, 1.5, y, ALU.add, ALU.mult))

            class Front:

                def __init__(self, t):
                    self.t = t
                    self.step, self.count = stepper(F.front_step, t, VF)

                def scale_x(self):
                    v.wait_ge(F.ssx_ready, self.t + 1)
                    rsqrt(self.step, fs[:, 1:2], fs[:, 2:3], fs[:, 3:4], fs[:, 0:1], 1.0 / D)
                    v.tensor_scalar(xt[:, :], xt[:, :], fs[:, 1:2], None, ALU.mult).then_inc(F.h_scaled, 1)

                def copy_hT(self):
                    v.wait_ge(F.h_turned, self.t + 1)
                    for b in range(2):
                        v.tensor_tensor(hT[:, 4 * b:4 * b + 4, :], heads(pm[b]), wide(gain1[:, 4 * b:4 * b + 4]),
                                        ALU.mult).then_inc(F.hT_ready, 1)

                def gate_inputs(self):
                    v.wait_ge(F.chunk_copied, 6 * self.t + 5)
                    self.step(v.tensor_tensor(fs[:, 4:8], tail[:, AL0:AL0 + H], dtb, ALU.add))
                    self.step(v.tensor_scalar(fs[:, 12:16], fs[:, 4:8], 0.0, None, ALU.max))
                    v.scalar_tensor_tensor(fs[:, 8:12], fs[:, 12:16], -2.0, fs[:, 4:8], ALU.mult,
                                           ALU.add).then_inc(F.u_ready, 1)

                def gate_outputs(self):
                    v.wait_ge(F.ln_ready, self.t + 1)
                    self.step(v.tensor_scalar(fs[:, 4:8], fs[:, 4:8], 0.0, None, ALU.max))
                    self.step(v.tensor_tensor(fs[:, 16:20], fs[:, 16:20], fs[:, 4:8], ALU.add))
                    v.wait_ge(F.tz_ready, self.t + 1)
                    v.tensor_tensor(fs[:, 20:24], fs[:, 16:20], neg_a, ALU.mult)
                    v.tensor_scalar(fs[:, 28:32], fs[:, 24:28], 0.5, 0.5, ALU.mult, ALU.add).then_inc(F.la_ready, 1)
                    v.wait_ge(F.hz_ready, self.t + 1)
                    v.scalar_tensor_tensor(gsz[:, :, :], gsz[:, :, :], 1.0,
                                           tail[:, Z0:Z0 + HP].rearrange("p (h n) -> p h n", h=H),
                                           ALU.add, ALU.mult).then_inc(F.gsz_ready, 1)

                def attention_norm(self):
                    v.wait_ge(F.swa_squared, self.t + 1)
                    self.step(v.tensor_reduce(fs[:, 32:42], qkg[:, :, :], AX_X, ALU.add))
                    rsqrt(self.step, fs[:, 42:52], fs[:, 52:62], fs[:, 62:72], fs[:, 32:42], 1.0 / DH)
                    v.wait_ge(F.swa_gained, self.t + 1)
                    v.tensor_tensor(qkn[:, 0:QH, :].rearrange("p (g kv) n -> p kv g n", kv=KVH),
                                    tail[:, SQ0:SK0].rearrange("p (kv g n) -> p kv g n", kv=KVH, g=GRP),
                                    fs[:, 42:42 + QH].rearrange("p (kv g) -> p kv g", kv=KVH).unsqueeze(3)
                                    .broadcast_to([P, KVH, GRP, DH]), ALU.mult)
                    v.tensor_tensor(qkn[:, QH:, :], tail[:, SK0:SV0].rearrange("p (h n) -> p h n", n=DH),
                                    wide(fs[:, 42 + QH:52], DH), ALU.mult).then_inc(F.qkn_ready, 1)

                def silu(self):
                    v.wait_ge(F.tanh_ready, self.t + 1)
                    v.scalar_tensor_tensor(qkvT[:, :, :], ctmp[:, :, :], 1.0, cv[:, :, :], ALU.add,
                                           ALU.mult).then_inc(F.qkvT_ready, 1)

            def front(t):
                f = Front(t)
                f.scale_x()
                f.copy_hT()
                f.gate_inputs()
                f.gate_outputs()
                f.attention_norm()
                f.silu()
                assert f.count[0] == VF, f.count

            class Late:

                def __init__(self, t):
                    self.t = t
                    self.step, self.count = stepper(B.late_step, t, VL)

                def add_x(self, n):
                    if n == 0:
                        v.wait_ge(L.xr_loaded, 16 * self.t + 16)
                    v.wait_ge(B.out_done, 2 * self.t + n + 1)
                    v.tensor_tensor(xr[:, 512 * n:512 * n + 512], xr[:, 512 * n:512 * n + 512], pm[6 + n][:, :],
                                    ALU.add).then_inc(B.xm_ready, 1)

                def norm(self):
                    v.wait_ge(B.ss2_ready, self.t + 1)
                    rsqrt(self.step, bs[:, 89:90], bs[:, 90:91], bs[:, 91:92], bs[:, 88:89], 1.0 / D)
                    v.tensor_scalar(y_mix[:, :], xr, bs[:, 89:90], None, ALU.mult).then_inc(B.hm_ready, 1)
                    assert self.count[0] == VL, self.count

                def copy_hT2(self):
                    v.wait_ge(B.hm_turned, self.t + 1)
                    for b in range(2):
                        v.tensor_tensor(hT2[:, 4 * b:4 * b + 4, :], heads(pm[6 + b]), wide(gain2[:, 4 * b:4 * b + 4]),
                                        ALU.mult).then_inc(B.hT2_ready, 1)

                def copy_logits(self):
                    v.wait_ge(B.logits_done, self.t + 1)
                    v.tensor_tensor(lg[:, bass.ds(self.t, 1), :], pm[6][:, 0:NL].unsqueeze(1), b_rt.unsqueeze(1),
                                    ALU.add).then_inc(B.lg_ready, 1)

            def late(t):
                f = Late(t)
                f.add_x(0)
                f.add_x(1)
                f.norm()
                f.copy_hT2()
                f.copy_logits()

            def body(t, nx_, pv_):
                nx = None if nx_ is None else Front(nx_)
                pv = None if pv_ is None else Late(pv_)
                step, count = stepper(B.back_step, t, VB)
                eg, ekl, cd = bs[:, 0:4], bs[:, 4:8], bs[:, 8:12]
                beta = bs[:, 92:96]

                def mask_a(l):
                    if l > 1:
                        v.wait_ge(B.y_done, 6 * t + l - 1)
                    v.tensor_tensor(aTm[:, l % 2, :, :], aT[:, :, :],
                                    level_mask[:, l + 1:l + 2, :].broadcast_to([P, H, P]), ALU.mult).then_inc(B.aTm_ready, 1)

                if nx:
                    nx.scale_x()
                    nx.copy_hT()
                v.wait_ge(B.small_done, t + 1)
                if later(t):
                    v.wait_ge(B.eg_ready, t)
                step(v.tensor_copy(bs[:, 12:16], pm[4][:, 8:12]))
                v.tensor_copy(bs[:, 20:24], pm[4][:, 12:16])
                v.tensor_copy(beta, fs[:, 28:32])
                v.tensor_tensor(bs[:, 16:20], pm[4][:, 12:16], bs[:, 12:16], ALU.subtract)
                step(v.tensor_tensor(dT[:, :, :], heads(pm[5]), wide(bs[:, 12:16]), ALU.subtract))
                v.tensor_scalar(dT[:, :, :], dT[:, :, :], 0.0, None, ALU.min).then_inc(B.diff_ready, 1)
                rsqrt(step, bs[:, 24:32], bs[:, 32:40], bs[:, 40:48], pm[4][:, 0:8], 1.0)
                v.tensor_tensor(kn[:, :, :], heads(pm[2]), wide(bs[:, 28:32]), ALU.mult).then_inc(B.kn_ready, 1)
                v.wait_ge(B.dT_exp, t + 1)
                step(v.tensor_tensor(dT[:, :, :], dT[:, :, :], upper[:, None, :].broadcast_to([P, H, P]), ALU.mult))
                if pv:
                    pv.add_x(0)
                    pv.add_x(1)
                v.wait_ge(B.kk_done, t + 1)
                step(v.tensor_tensor(aT[:, :, :], heads(pm[3]), dT[:, :, :], ALU.mult))
                v.tensor_tensor(aT[:, :, :], aT[:, :, :], wide(beta), ALU.mult).then_inc(B.aT_ready, 1)
                v.wait_ge(B.aT_ready, t + 1)
                step(v.tensor_tensor(XT[:, :, :], aT[:, :, :], level_mask[:, 0:1, :].broadcast_to([P, H, P]),
                                     ALU.mult))
                v.tensor_tensor(XT[:, :, :], ident[:, None, :].broadcast_to([P, H, P]), XT[:, :, :],
                                ALU.subtract).then_inc(B.xT0_ready, 1)
                mask_a(0)
                mask_a(1)
                v.wait_ge(B.qk_done, t + 1)
                v.tensor_tensor(qkT[:, :, :], heads(pm[5]), dT[:, :, :], ALU.mult).then_inc(B.qkT_ready, 1)
                if pv:
                    pv.norm()
                    pv.copy_hT2()
                for l in range(len(LEVELS)):
                    v.wait_ge(B.z_done, 6 * t + l + 1)
                    if l < len(LEVELS) - 1:
                        v.tensor_tensor(X[:, :, :], X[:, :, :], heads(pm[2]), ALU.subtract).then_inc(B.x_updated, 1)
                    else:
                        v.tensor_tensor(o[:, :, :], heads(pm[2]), wide(eg), ALU.mult)
                    if l < len(LEVELS) - 2:
                        mask_a(l + 2)
                    v.wait_ge(B.zt_done, 6 * t + l + 1)
                    v.tensor_tensor(XT[:, :, :], XT[:, :, :], heads(pm[5]), ALU.subtract).then_inc(B.xT_updated, 1)
                    if l == 0:
                        if pv:
                            pv.copy_logits()
                        v.wait_ge(B.ks_done, t + 1)
                        v.wait_ge(B.eg_ready, t + 1)
                        v.wait_ge(B.vt_ready, t + 1)
                        step(v.tensor_tensor(V[:, :, :], heads(pm[4]), wide(eg), ALU.mult))
                        v.tensor_tensor(r[:, :, :], vt[:, :, :], V[:, :, :], ALU.subtract).then_inc(B.r_ready, 1)
                    if l == 2:
                        v.wait_ge(B.scores_done, t + 1)
                        if later(t):
                            v.wait_ge(L.mid_stored, 32 * t)
                        top = bs[:, 64:72]
                        for kv in range(KVH):
                            src = heads(pm[6 + kv])
                            if not later(t):
                                v.tensor_tensor(sc[:, 4 * kv:4 * kv + 4, :], src,
                                                key_mask[:, None, :].broadcast_to([P, GRP, P]),
                                                ALU.add).then_inc(L.masked, 1)
                                v.wait_ge(L.masked, kv + 1)
                                src = sc[:, 4 * kv:4 * kv + 4, :]
                            ins = v.tensor_reduce(top[:, 4 * kv:4 * kv + 4], src, AX_X, ALU.max)
                        ins.then_inc(B.top_found, 1)
                        v.wait_ge(B.top_found, t + 1)
                        step(v.tensor_tensor(top, top, sink, ALU.max))
                        for kv in range(KVH):
                            src = sc[:, 4 * kv:4 * kv + 4, :] if not later(t) else heads(pm[6 + kv])
                            v.tensor_tensor(sc[:, 4 * kv:4 * kv + 4, :], src, wide(top[:, 4 * kv:4 * kv + 4]),
                                            ALU.subtract)
                        v.tensor_tensor(bs[:, 48:56], sink, top, ALU.subtract).then_inc(B.sc_ready, 1)
                v.wait_ge(B.v0_done, t + 1)
                v.tensor_tensor(V[:, :, :], heads(pm[3]), wide(beta), ALU.mult).then_inc(B.v_ready, 1)
                step(v.tensor_tensor(S[:, :, :], S[:, :, :], wide(cd), ALU.mult))
                v.wait_ge(B.pv_done, t + 1)
                v.wait_ge(B.sink_exp, t + 1)
                pv_out = [pm[6 + kv][:, 0:GRP * (DH + 1)].rearrange("p (g n) -> p g n", n=DH + 1) for kv in range(KVH)]
                for kv in range(KVH):
                    ins = v.tensor_tensor(bs[:, 96 + 4 * kv:100 + 4 * kv], pv_out[kv][:, :, DH],
                                          bs[:, 56 + 4 * kv:60 + 4 * kv], ALU.add)
                step(ins)
                step(v.reciprocal(bs[:, 104:112], bs[:, 96:104]))
                for kv in range(KVH):
                    ins = v.tensor_tensor(
                        y_mix[:, HP + 256 * kv:HP + 256 * kv + 256].rearrange("p (g n) -> p g n", n=DH),
                        pv_out[kv][:, :, 0:DH], wide(bs[:, 104 + 4 * kv:108 + 4 * kv], DH), ALU.mult)
                ins.then_inc(B.yb_ready, 1)
                v.wait_ge(B.s_done, t + 1)
                v.tensor_tensor(S[:, :, :], S[:, :, :], heads(pm[5]), ALU.add).then_inc(B.s_updated, 1)
                v.wait_ge(B.o2_done, t + 1)
                step(v.tensor_tensor(o[:, :, :], o[:, :, :], heads(pm[4]), ALU.add))
                v.scalar_tensor_tensor(o[:, :, :], o[:, :, :], float(P) ** -0.5, wide(bs[:, 24:28]), ALU.mult,
                                       ALU.mult).then_inc(B.o_ready, 1)
                v.wait_ge(B.o_ready, t + 1)
                step(v.tensor_tensor(o2[:, :, :], o[:, :, :], o[:, :, :], ALU.mult))
                step(v.tensor_reduce(bs[:, 72:76], o2[:, :, :], AX_X, ALU.add))
                rsqrt(step, bs[:, 76:80], bs[:, 80:84], bs[:, 84:88], bs[:, 72:76], 1.0 / P)
                step(v.tensor_tensor(o[:, :, :], o[:, :, :], wide(bs[:, 76:80]), ALU.mult))
                v.tensor_tensor(y_mix[:, 0:HP].rearrange("p (h n) -> p h n", h=H), o[:, :, :], gsz[:, :, :],
                                ALU.mult).then_inc(B.ya_ready, 1)
                if nx:
                    nx.gate_inputs()
                    nx.silu()
                    nx.gate_outputs()
                    nx.attention_norm()
                    assert nx.count[0] == VF, nx.count
                assert count[0] == VB, count

            v.wait_ge(L.consts_loaded, 16 * NSMALL)
            v.wait_ge(L.weights_ready, 1)
            v.tensor_scalar(neg_a, neg_a, -1.0, None, ALU.mult)
            v.tensor_scalar(g_out, g_out, 0.5, None, ALU.mult)
            v.tensor_scalar(sink, sink, DH ** 0.5, None, ALU.mult)
            v.tensor_scalar(cw[:, :, :], cw[:, :, :], 0.5, None, ALU.mult).then_inc(L.dve_consts, 1)
            v.wait_ge(L.dve_consts, 1)
            v.wait_ge(L.masks_made, 1)
            run_tiles(front, body, late, v)
            v.wait_ge(B.lg_ready, NT)
            v.wait_ge(R.iotas, 1)
            step, count = stepper(R.route_step, 0, 0)

            def tt(dst, a, b, op):
                step(v.tensor_tensor(dst, a, b, op))

            def over_last(ap2, n):
                return ap2.unsqueeze(len(ap2.shape)).broadcast_to(list(ap2.shape) + [n])

            def first_only(hot):
                step(v.tensor_copy(seen, hot[:, :, 0]))
                for i in range(1, hot.shape[2]):
                    tt(hot[:, :, i], hot[:, :, i], seen, ALU.is_gt)
                    tt(seen, seen, hot[:, :, i], ALU.max)

            gl, el = lg[:, :, 0:GROUPS], lg[:, :, GROUPS:NL].rearrange("p t (g e) -> p t g e", g=GROUPS)
            step(v.tensor_reduce(gmax, gl, AX_X, ALU.max))
            tt(ex[:, 0:NT * GROUPS].rearrange("p (t g) -> p t g", g=GROUPS), gl, over_last(gmax, GROUPS), ALU.subtract)
            tt(og, gl, over_last(gmax, GROUPS), ALU.is_equal)
            first_only(og)
            tt(prod, el, over_last(og, EPG), ALU.mult)
            step(v.tensor_reduce(es, prod.rearrange("p t g e -> p t e g"), AX_X, ALU.add))
            step(v.tensor_reduce(m1, es, AX_X, ALU.max))
            tt(e1, es, over_last(m1, EPG), ALU.is_equal)
            first_only(e1)
            step(v.scalar_tensor_tensor(es, e1, -BIG, es, ALU.mult, ALU.add))
            step(v.tensor_reduce(m2, es, AX_X, ALU.max))
            tt(e2, es, over_last(m2, EPG), ALU.is_equal)
            first_only(e2)
            v.tensor_tensor(ex[:, NT * GROUPS:], m2, m1, ALU.subtract).then_inc(R.exp_in, 1)
            for pick, e in ((pick1, e1), (pick2, e2)):
                tt(pick, over_last(og, EPG), e.unsqueeze(2).broadcast_to([P, NT, GROUPS, EPG]), ALU.mult)
            v.tensor_tensor(both_picks, pick1, pick2, ALU.add).then_inc(R.picks, 1)
            v.wait_ge(R.exp_out, 1)
            step(v.tensor_reduce(sump, ex[:, 0:NT * GROUPS].rearrange("p (t g) -> p t g", g=GROUPS), AX_X, ALU.add))
            step(v.scalar_tensor_tensor(sump, ex[:, NT * GROUPS:], 1.0, sump, ALU.add, ALU.mult))
            step(v.reciprocal(gate1, sump))
            tt(gate2, gate1, ex[:, NT * GROUPS:], ALU.mult)
            v.wait_ge(R.counts, 1)
            step(v.memset(run[:, 0, :], 0.0))
            tot = pm[0][:, P:2 * P].rearrange("p (t e) -> p t e", e=NE)
            for t in range(NT):
                tt(run[:, t + 1, :], tot[:, t, :], run[:, t, :], ALU.add)
            tt(slot, pm[0][:, 0:P].rearrange("p (t e) -> p t e", e=NE), run[:, 0:NT, :], ALU.add)
            tt(over, over_last(run[:, NT, :], NT), step_f.unsqueeze(1).broadcast_to([P, NE, NT]), ALU.is_gt)
            step(v.tensor_reduce(tiles_of, over, AX_X, ALU.add))
            step(v.tensor_tensor_scan(tiles_to, ones[:, 0:NE], tiles_of, 0.0, ALU.mult, ALU.add))
            tt(base, tiles_to, tiles_of, ALU.subtract)
            step(v.scalar_tensor_tensor(slot, base.unsqueeze(1).broadcast_to([P, NT, NE]), float(P), slot,
                                        ALU.mult, ALU.add))
            for c, pick in enumerate((pick1, pick2)):
                tt(prod, pick, slot.rearrange("p t (g e) -> p t g e", g=GROUPS), ALU.mult)
                step(v.tensor_reduce(slots[:, c * NT:(c + 1) * NT], prod.rearrange("p t g e -> p t (g e)"), AX_X, ALU.add))
            tt(past[0:1], tiles_to[0:1].unsqueeze(1).broadcast_to([1, SLOT_TILES + 1, NE]),
               over_last(iota_f[0:1, 0:SLOT_TILES + 1], NE), ALU.is_le)
            step(v.tensor_reduce(texp_f[0:1], past[0:1], AX_X, ALU.add))
            step(v.tensor_scalar(texp_f[0:1], texp_f[0:1], float(NE - 1), None, ALU.min))
            step(v.tensor_copy(texp[0:1], texp_f[0:1]))
            step(v.tensor_copy(slots_i, slots))
            step(v.tensor_scalar(mod_i, slots_i, P - 1, None, ALU.bitwise_and))
            step(v.tensor_scalar(div_i, slots_i, P.bit_length() - 1, None, ALU.logical_shift_right))
            step(v.tensor_copy(mod_f, mod_i))
            v.tensor_copy(div_f, div_i).then_inc(R.ready, 1)
            v.wait_ge(R.ready, 1)
            for u in range(TOPK * NT):
                v.tensor_scalar(hot_mod[u], iota_f, mod_f[:, u:u + 1], tok_f[:, u % NT:u % NT + 1], ALU.is_equal, ALU.mult)
                ins = v.tensor_scalar(hot_div[:, u, :], iota_f[:, 0:32], div_f[:, u:u + 1], None, ALU.is_equal)
            ins.then_inc(R.hots, 1)
            v.wait_ge(R.idx_summed, 1)
            v.tensor_copy(idx, pm[1][:, 0:32]).then_inc(R.idx_ready, 1)

            def copy_rows(m, b, u):
                v.wait_ge(M.turned, m + 1)
                for n in range(2):
                    if n == 0 and (not isinstance(m, int) or m > 1):
                        v.wait_ge(M.gu_done, m - 1)
                    v.tensor_tensor(hgT[b][:, 4 * n:4 * n + 4, :], heads(pm[n]), wide(gain2[:, 4 * n:4 * n + 4]),
                                    ALU.mult).then_inc(M.hT_ready, 1)

            def swiglu(m, b, u):
                v.wait_ge(M.tanh_ready, m + 1)
                if later(m):
                    v.wait_ge(M.glu_turned, m)
                v.scalar_tensor_tensor(tnh, tnh, 1.0, pm[2 + b][:, 0:DE], ALU.add, ALU.mult).then_inc(M.glu_step, 1)
                v.wait_ge(M.glu_step, m + 1)
                v.scalar_tensor_tensor(glu, tnh, 0.5, pm[2 + b][:, DE:2 * DE], ALU.mult, ALU.mult).then_inc(M.glu_ready, 1)

            def copy_out(m, b, u):
                v.wait_ge(M.glu_turned, m + 1)
                v.tensor_copy(gluT, pm[4][:, 0:DE].rearrange("p (k n) -> p k n", n=P)).then_inc(M.gluT_ready, 1)
                v.wait_ge(M.down_done, 2 * m + 1)
                if not isinstance(u, int) or u > 0:
                    v.wait_ge(y_stored[b], 16 * u)
                v.tensor_copy(yo[b][:, 0:512], pm[6][:, :]).then_inc(M.y0_ready, 1)

            def step_m(m, b, u):
                if not isinstance(m, int) or m < SLOT_TILES - 1:
                    copy_rows(m + 1, 1 - b, u + b)
                if later(m):
                    copy_out(m - 1, 1 - b, u - 1 + b)
                swiglu(m, b, u)

            copy_rows(0, 0, 0)
            run_slots(v, step_m, lambda: copy_out(SLOT_TILES - 1, 0, SLOT_TILES // 2))
            for t in range(NT):
                b, k = t % 2, 16 * (t // 2) + 16
                v.wait_ge(m_loaded[b], k)
                v.wait_ge(a_loaded[b], k)
                v.scalar_tensor_tensor(out_x[b], out_a[b], gate1[:, t:t + 1], out_x[b], ALU.mult, ALU.add).then_inc(M.half_summed, 1)
                v.wait_ge(M.half_summed, t + 1)
                v.wait_ge(b_loaded[b], k)
                v.scalar_tensor_tensor(out_x[b], out_b[b], gate2[:, t:t + 1], out_x[b], ALU.mult, ALU.add).then_inc(M.summed, 1)

        @block.gpsimd
        def _(g):
            made = ctx.enter_context(nc.semaphore("pool_made"))
            count = [0]

            def step(ins):
                count[0] += 1
                ins.then_inc(made, 1)
                g.wait_ge(made, count[0])

            def select(m, pattern, base, cm, op=ALU.is_ge, fill=0.0):
                step(g.affine_select(out=m, in_=m, pattern=pattern, compare_op=op, fill=fill, base=base,
                                     channel_multiplier=cm))

            step(g.memset(ones[:, :], 1.0))
            step(g.memset(ident[:, :], 0.0))
            select(ident[:, :], [[-1, P]], 0, 1, ALU.not_equal, 1.0)
            step(g.memset(upper[:, :], 1.0))
            select(upper[:, :], [[1, P]], 0, -1)
            step(g.memset(upper_strict[:, :], 1.0))
            select(upper_strict[:, :], [[1, P]], -1, -1)
            step(g.memset(level_mask[:, :, :], 1.0))
            for n, s_ in enumerate([1] + LEVELS):
                m = level_mask[:, n, :].rearrange("p (b r) -> p b r", r=2 * s_)
                nb = P // (2 * s_)
                select(m, [[-2 * s_, nb], [0, 2 * s_]], 0, 1)
                select(m, [[2 * s_, nb], [0, 2 * s_]], s_ - 1, -1)
                select(m, [[0, nb], [1, 2 * s_]], -s_, 0)
            step(g.memset(key_mask[:, :], 0.0))
            step(g.memset(key_mask[0:CH, CH:P], -BIG))
            step(g.memset(S[:, :, :], 0.0))
            step(g.memset(vWin[:, :, :, :], 0.0))
            step(g.memset(vWin[:, :, :, DH:DH + 1], 1.0))
            step(g.memset(kWin[:, :, :], 0.0))
            g.memset(ci[:, :, :], 0.0).then_inc(L.masks_made, 1)
            g.wait_ge(L.masks_made, 1)
            g.wait_ge(L.dve_consts, 1)

            def copy(dst, src):
                p, n = src.start_partition(), src.shape
                one = ones[p:p + n[0], 0:1] if len(n) == 2 else ones[p:p + n[0], 0:1].unsqueeze(2)
                return g.tensor_tensor(dst, src, one.broadcast_to(list(n)), ALU.mult)

            def halo(t):
                if later(t):
                    g.wait_ge(F.conv_done, t)
                copy(ci[:, :, 0:HALO], ci[:, :, P:P + HALO]).then_inc(F.halo_ready, 1)

            def conv(t):
                g.wait_ge(F.ci_copied, 3 * t + 3)
                if later(t):
                    g.wait_ge(B.xT_updated, 6 * t - 2)
                g.tensor_tensor(cv, ci[:, :, 0:P], wide(cw[:, 0, :]), ALU.mult)
                for j in range(1, KW):
                    g.tensor_tensor(ctmp[:, :, :], ci[:, :, j:j + P], wide(cw[:, j, :]), ALU.mult).then_inc(F.conv_step, 1)
                    g.wait_ge(F.conv_step, (2 * KW - 3) * t + 2 * j - 1)
                    ins = g.tensor_tensor(cv, cv, ctmp[:, :, :], ALU.add)
                    if j < KW - 1:
                        ins.then_inc(F.conv_step, 1)
                        g.wait_ge(F.conv_step, (2 * KW - 3) * t + 2 * j)
                ins.then_inc(F.conv_done, 1)

            def front_tail(t):
                g.wait_ge(F.swa_squared, t + 1)
                qk_in = tail[:, SQ0:SQ0 + QK].rearrange("p (h n) -> p h n", n=DH)
                g.tensor_tensor(qk_in[:, 0:QH, :], qk_in[:, 0:QH, :],
                                gqk[:, None, 0:DH].broadcast_to([P, QH, DH]), ALU.mult)
                g.tensor_tensor(qk_in[:, QH:, :], qk_in[:, QH:, :],
                                gqk[:, None, DH:2 * DH].broadcast_to([P, KVH, DH]), ALU.mult).then_inc(F.swa_gained, 1)
                z = tail[:, Z0:Z0 + HP].rearrange("p (h n) -> p h n", h=H)
                g.wait_ge(F.tz_ready, t + 1)
                g.tensor_tensor(z, z, g_out[:, None, :].broadcast_to([P, H, P]), ALU.mult).then_inc(F.hz_ready, 1)

            def front(t):
                halo(t)
                conv(t)
                front_tail(t)

            def body(t, nx, pv):
                if later(t):
                    g.wait_ge(B.scores_done, t)
                copy(kWin[:, 1, :], kWin[:, 2, :]).then_inc(B.kOld_ready, 1)
                g.wait_ge(B.kOld_ready, t + 1)
                if later(t):
                    g.wait_ge(B.pv_done, t)
                copy(vWin[CH:P, 0, :, 0:DH], vWin[CH:P, 1, :, 0:DH]).then_inc(B.vOld_ready, 1)
                g.wait_ge(B.vOld_ready, t + 1)
                vin = tail[:, SV0:SV0 + KVH * DH].rearrange("p (h n) -> p h n", n=DH)
                copy(vWin[:, 1, :, 0:DH], vin)
                copy(vWin[0:CH, 0, :, 0:DH], vin[0:CH]).then_inc(B.vWin_ready, 1)
                g.wait_ge(B.kn_ready, t + 1)
                g.wait_ge(B.eg_ready, t + 1)
                g.wait_ge(B.kn_turned, t + 1)
                g.tensor_tensor(kd[:, :, :], kn[:, :, :], wide(bs[:, 4:8]), ALU.mult).then_inc(B.kd_ready, 1)
                if nx is not None:
                    halo(nx)
                    conv(nx)
                    front_tail(nx)

            run_tiles(front, body, lambda t: None, g)
            g.wait_ge(B.lg_ready, NT)
            step(g.iota(iota_i, [[1, P]], base=0, channel_multiplier=0))
            step(g.tensor_copy(iota_f, iota_i))
            step(g.iota(iota_i[:, 0:NT], [[P, NT]], base=0, channel_multiplier=0))
            step(g.tensor_copy(step_f, iota_i[:, 0:NT]))
            step(g.iota(iota_i[:, 0:NT], [[P, NT]], base=0, channel_multiplier=1))
            g.tensor_copy(tok_f, iota_i[:, 0:NT]).then_inc(R.iotas, 1)

            g.wait_ge(L.mid_stored, 32 * NT)
            g.wait_ge(R.idx_ready, 1)
            for m in range(SLOT_TILES):
                if m > 1:
                    g.wait_ge(M.turned, m - 1)
                g.indirect_dma_start(hg[m % 2], None, h_mid,
                                     bass.IndirectOffsetOnAxis(idx[:, m:m + 1], 0)).then_inc(gathered[m % 2], 16)
            for b in range(2):
                g.wait_ge(y_stored[b], 16 * ((SLOT_TILES + 1 - b) // 2))
            for t in range(NT):
                b = t % 2
                if t > 1:
                    g.wait_ge(M.summed, t - 1)
                g.indirect_dma_start(out_a[b], None, y_slots, bass.IndirectOffsetOnAxis(slots_i[:, t:t + 1], 0)).then_inc(a_loaded[b], 16)
                g.indirect_dma_start(out_b[b], None, y_slots, bass.IndirectOffsetOnAxis(slots_i[:, NT + t:NT + t + 1], 0)).then_inc(b_loaded[b], 16)


_INS = ["x", "attn_norm_g", "w_in", "conv_w", "gdn_a_log", "gdn_dt_bias", "gdn_out_norm_g", "swa_q_norm_g",
        "swa_k_norm_g", "swa_sinks", "w_out", "ffn_norm_g", "w_group", "b_group", "w_expert", "b_expert",
        "w_gate_up", "w_down"]


def kernel(**inputs):
    import concourse.bacc as bacc
    from concourse.bass_utils import run_bass_kernel_spmd

    nc = bacc.Bacc("TRN2", target_bir_lowering=False, num_devices=1)
    arrays, args = {}, []
    for name in _INS:
        a = np.ascontiguousarray(inputs[name])
        arrays[f"in_{name}"] = a
        args.append(nc.dram_tensor(f"in_{name}", a.shape, mybir.dt.from_np(a.dtype), kind="ExternalInput").ap())
    out = nc.dram_tensor("out", [1, T, D], F32, kind="ExternalOutput").ap()
    build(nc, *args, out)
    return run_bass_kernel_spmd(nc, [arrays], core_ids=[0]).results[0]["out"]
```
